# Optimizing a Trainium2 kernel written in Bass

```python
import math
import jax, jax.numpy as jnp
from jax import lax
import numpy as np

D_MODEL = 1024
BATCH = 1
SEQ = 1024
DEPTH = 1

PLE_DIM = 256
ATTN_HEADS = 16
HEAD_DIM = 64
ATTN_WIDTH = ATTN_HEADS * HEAD_DIM
POOL_WINDOWS = (2, 4, 8, 16)
N_POOL_GROUPS = len(POOL_WINDOWS)
POOL_GROUP_DIM = 256
POOL_WIDTH = N_POOL_GROUPS * POOL_GROUP_DIM
MIX_WIDTH = ATTN_WIDTH + POOL_WIDTH
Q_BLOCK = 128
EPS = 1e-6
SPLIT_SIZES = (ATTN_WIDTH, ATTN_WIDTH, ATTN_WIDTH, ATTN_WIDTH, ATTN_HEADS, POOL_WIDTH, POOL_WIDTH)
IN_COLS = sum(SPLIT_SIZES)
SPLIT_POINTS = tuple(int(v) for v in np.cumsum(SPLIT_SIZES)[:-1])

kernel_name = "hymba_fox_pool_hybrid"

def rms_norm(x, g):
    xf = x.astype(jnp.float32)
    y = xf * lax.rsqrt(jnp.mean(xf * xf, axis=-1, keepdims=True) + EPS)
    return (y * g.astype(jnp.float32)).astype(x.dtype)

def multi_scale_pool(u, w_pool, pool_scale):
    B, S, _ = u.shape
    ug = u.reshape(B, S, N_POOL_GROUPS, POOL_GROUP_DIM).astype(jnp.float32)
    cs = jnp.cumsum(ug, axis=1)
    pos = jnp.arange(1, S + 1, dtype=jnp.float32)
    outs = []
    for g, w in enumerate(POOL_WINDOWS):
        c = cs[:, :, g]
        shifted = jnp.pad(c, ((0, 0), (w, 0), (0, 0)))[:, :S]
        count = jnp.minimum(pos, float(w))[None, :, None]
        outs.append((c - shifted) / count - ug[:, :, g])
    pooled = jnp.stack(outs, axis=2).astype(u.dtype)
    mixed = jnp.einsum('bsgc,gcd->bsgd', pooled, w_pool)
    return mixed.reshape(B, S, POOL_WIDTH) * pool_scale

def forgetting_attention(q, k, v, log_f):
    B, S, H, Dh = q.shape
    scale = 1.0 / math.sqrt(Dh)
    c = jnp.cumsum(log_f, axis=1).transpose(0, 2, 1)
    qh = q.transpose(0, 2, 1, 3)
    kh = k.transpose(0, 2, 1, 3)
    vh = v.transpose(0, 2, 1, 3)
    tri = jnp.tril(jnp.ones((Q_BLOCK, Q_BLOCK), dtype=bool))
    outs = []
    for i in range(S // Q_BLOCK):
        q0 = i * Q_BLOCK
        end = q0 + Q_BLOCK
        qb = qh[:, :, q0:end]
        kb = kh[:, :, :end]
        vb = vh[:, :, :end]
        s = jnp.einsum('bhqd,bhkd->bhqk', qb, kb,
                       preferred_element_type=jnp.float32) * scale
        s = s + c[:, :, q0:end, None] - c[:, :, None, :end]
        mask = jnp.concatenate([jnp.ones((Q_BLOCK, q0), dtype=bool), tri], axis=1)
        s = jnp.where(mask[None, None], s, -jnp.inf)
        pr = jax.nn.softmax(s, axis=-1)
        outs.append(jnp.einsum('bhqk,bhkd->bhqd', pr.astype(v.dtype), vb))
    o = jnp.concatenate(outs, axis=2)
    return o.transpose(0, 2, 1, 3)

def setup_inputs(seed: int = 0) -> dict:
    key = jax.random.key(seed)
    ks = jax.random.split(key, 12)
    f32 = jnp.float32
    x = jax.random.normal(ks[0], (BATCH, SEQ, D_MODEL), f32)
    p = jax.random.normal(ks[1], (DEPTH, BATCH, SEQ, PLE_DIM), f32)
    norm_pre = 1.0 + 0.05 * jax.random.normal(ks[2], (DEPTH, D_MODEL), f32)
    norm_post = 1.0 + 0.05 * jax.random.normal(ks[3], (DEPTH, D_MODEL), f32)
    w_in = jax.random.normal(ks[4], (DEPTH, D_MODEL, IN_COLS), f32) * D_MODEL ** -0.5
    b_f = 3.0 + 0.5 * jax.random.normal(ks[5], (DEPTH, ATTN_HEADS), f32)
    w_pool = jax.random.normal(ks[6], (DEPTH, N_POOL_GROUPS, POOL_GROUP_DIM, POOL_GROUP_DIM), f32) * POOL_GROUP_DIM ** -0.5
    pool_scale = 1.0 + 0.1 * jax.random.normal(ks[7], (DEPTH, POOL_WIDTH), f32)
    w_out = jax.random.normal(ks[8], (DEPTH, MIX_WIDTH, D_MODEL), f32) * MIX_WIDTH ** -0.5
    w_pg = jax.random.normal(ks[9], (DEPTH, D_MODEL, D_MODEL), f32) * D_MODEL ** -0.5
    w_pe = jax.random.normal(ks[10], (DEPTH, PLE_DIM, D_MODEL), f32) * (0.5 * PLE_DIM ** -0.5)
    return {"x": x, "p": p, "norm_pre": norm_pre, "norm_post": norm_post,
            "w_in": w_in, "b_f": b_f, "w_pool": w_pool, "pool_scale": pool_scale,
            "w_out": w_out, "w_pg": w_pg, "w_pe": w_pe}

def reference(x, p, norm_pre, norm_post, w_in, b_f, w_pool, pool_scale, w_out, w_pg, w_pe):
    B, S, _ = x.shape
    h = x
    for i in range(DEPTH):
        hn = rms_norm(h, norm_pre[i])
        proj = hn @ w_in[i]
        q, k, v, z_attn, f_logit, u_pool, z_pool = jnp.split(proj, SPLIT_POINTS, axis=-1)
        log_f = jax.nn.log_sigmoid(f_logit.astype(jnp.float32) + b_f[i].astype(jnp.float32))
        attn = forgetting_attention(
            q.reshape(B, S, ATTN_HEADS, HEAD_DIM),
            k.reshape(B, S, ATTN_HEADS, HEAD_DIM),
            v.reshape(B, S, ATTN_HEADS, HEAD_DIM), log_f)
        attn = attn.reshape(B, S, ATTN_WIDTH) * jax.nn.silu(z_attn)
        pool = multi_scale_pool(u_pool, w_pool[i], pool_scale[i]) * jax.nn.silu(z_pool)
        mix = jnp.concatenate([attn, pool], axis=-1) @ w_out[i]
        h = h + rms_norm(mix, norm_post[i])
        gate = jax.nn.sigmoid(h @ w_pg[i])
        h = h + gate * (p[i] @ w_pe[i])
    return h


_drawn_inputs = setup_inputs


def setup_inputs(seed=0):
    import zlib

    import numpy as np

    out = dict(_drawn_inputs(seed))
    spreads = {}
    factors = {}
    for name, (base, spread) in spreads.items():
        noise = np.random.default_rng([zlib.crc32(name.encode()), seed]).standard_normal(out[name].shape)
        drawn = base * np.exp(spread * noise) if base else spread * noise
        out[name] = __import__('jax').numpy.asarray(drawn.astype(out[name].dtype))
    for name, factor in factors.items():
        out[name] = (out[name] * factor).astype(out[name].dtype)
    return out
```

```python
from contextlib import ExitStack

import concourse.bass as bass
from concourse import mybir

F32 = mybir.dt.float32
F32R = mybir.dt.float32r
BF16 = mybir.dt.bfloat16
ACT = mybir.ActivationFunctionType
ALU = mybir.AluOpType

P = 128
D = 1024
S = 1024
KB = D // P
TB = S // P
HALF = 512
HEADS = 16
DH = 64
PAIRS = HEADS // 2
WINDOWS = (2, 4, 8, 16)
GROUPS = len(WINDOWS)
PAD = max(WINDOWS)
PLE = 256
PB = PLE // P
EPS = 1e-6
SCALE = DH ** -0.5
MASKED = -1e30

COL_Q, COL_K, COL_V, COL_Z = 0, D, 2 * D, 3 * D
COL_F = 4 * D
COL_U = COL_F + HEADS
COL_ZP = COL_U + D

CHUNK_OUT = 1 + 4 * (GROUPS + PAIRS)
CHUNK_PG = CHUNK_OUT + 2 * KB
HALF_OUT = 2 + 8 * (GROUPS + PAIRS)

TILES = 2 * TB
STEPS = TILES + 3
QUADS = {}
for _n in range(TILES):
    for _q in range(1 if _n % TB < 4 else 2):
        QUADS[(_n, _q)] = 2 + len(QUADS)
NQUADS = 2 + len(QUADS)
PIECES = [3, 2, 1, 1, 1, 2, 2, 2, 2, 2, 1, 1, 1, 2, 2, 2, 2, 2, 1]
assert len(PIECES) == STEPS and sum(PIECES) == 4 * 2 * (KB // 2)


def pieces(n):
    at = sum(PIECES[:n])
    return [(i // 8, i // 4 % 2, 2 * (i % 4)) for i in range(at, at + PIECES[n])]


def quad_blocks(n, q):
    return range(4 * q, min(4 * q + 4, n % TB + 1))


def hymba_kernel(nc, x, p, norm_pre, norm_post, w_in, b_f, w_pool, pool_scale, w_out, w_pg, w_pe, ramp, out):
    with ExitStack() as ctx:
        def sem(name):
            return ctx.enter_context(nc.semaphore(name))

        def psum(name, shape):
            return ctx.enter_context(nc.psum_tensor(name, shape, F32))

        base = nc.sbuf_base
        end = nc.sbuf_usable_end
        place = [(base + 31) // 32 * 32]

        def at(name, shape, dt, offset):
            n = 2 if dt == BF16 else 4
            for d in shape[1:]:
                n *= d
            n = (n + 31) // 32 * 32
            assert offset + n <= end, (name, offset + n, end)
            return nc.alloc_sbuf_tensor_at(name, shape, dt, offset=offset), offset + n

        def sb(name, shape, dt=F32):
            t, place[0] = at(name, shape, dt, place[0])
            return t

        hn_h = sb("hn_h", [P, KB, S], F32R)
        hn_l = sb("hn_l", [P, KB, S], F32R)
        w_raw = sb("w_raw", [P, 2, KB, P])
        w_h = sb("w_h", [P, 2, KB, P], F32R)
        w_l = sb("w_l", [P, 2, KB, P], F32R)
        gate = sb("gate", [P, 2, S])
        vT = sb("vT", [P, S])
        ident = sb("ident", [P, P])
        ident_b = sb("ident_b", [P, P], BF16)
        mask_b = sb("mask_b", [P, P], BF16)
        ones = sb("ones", [P, P])
        gpost = sb("gpost", [P, KB])
        pscale = sb("pscale", [P, KB])
        ramp_sb = sb("ramp_sb", [P, GROUPS, PAD])
        bf_sb = sb("bf_sb", [HEADS, 1])
        ssq = sb("ssq", [P, TB])
        rms = sb("rms", [P, TB])
        rinv = sb("rinv", [P, TB])
        eps_sb = sb("eps_sb", [P, 1])
        wait_sb = sb("wait_sb", [P, 1])
        neg_max = sb("neg_max", [P, 3])
        den = sb("den", [P, 3])
        rden = sb("rden", [P, 3])
        pv_tmp = sb("pv_tmp", [P, 2, 2 * P])
        region = place[0]
        q_h = sb("q_h", [P, 2, S], F32R)
        q_l = sb("q_l", [P, 2, S], F32R)
        k_h = sb("k_h", [P, 2, S], F32R)
        k_l = sb("k_l", [P, 2, S], F32R)
        pt_h = [sb("pt0_h", [P, 6, 2 * P], F32R), None]
        pt_l = [sb("pt0_l", [P, 6, 2 * P], F32R), None]
        pt_h[1] = sb("pt1_h", [P, 8, 2 * P], F32R)
        pt_l[1] = sb("pt1_l", [P, 8, 2 * P], F32R)
        v_s = sb("v_s", [P, TB, 2, P], F32R)
        late = place[0]
        e_sb = sb("e_sb", [P, 3, S + PAD])
        cb = sb("cb", [P, 2, S])
        x_all, _ = at("x_all", [P, TB, D], F32, region)
        pooled_h = pt_h[1][:].rearrange("p b c -> p (b c)").rearrange("p (c s) -> p c s", c=2)
        pooled_l = pt_l[1][:].rearrange("p b c -> p (b c)").rearrange("p (c s) -> p c s", c=2)
        wp_h = pt_h[0][:, 0:2, :]
        wp_l = pt_l[0][:, 0:2, :]
        wp_raw = cb[:, 1, 0:2 * 256].rearrange("p (c n) -> p c n", c=2)
        g_pre = cb[:, 0, :]
        at_h, o1 = at("at_h", [P, KB, S], F32R, region)
        at_l, _ = at("at_l", [P, KB, S], F32R, o1)
        xT, _ = at("xT", [P, KB, S], F32, region)
        pT_h, o2 = at("pT_h", [P, PB, S], F32R, o1)
        pT_l, o2 = at("pT_l", [P, PB, S], F32R, o2)
        p_raw, o2 = at("p_raw", [P, TB // 2, PLE], F32, o2)
        x_raw, o2 = at("x_raw", [P, 2, D], F32, o2)
        pe_raw, o2 = at("pe_raw", [P, 2, PB, P], F32, o2)
        pe_h, o2 = at("pe_h", [P, 2, PB, P], F32R, o2)
        pe_l, o2 = at("pe_l", [P, 2, PB, P], F32R, o2)
        assert o2 <= late
        mixed, _ = at("mixed", [P, KB, S], F32, late)

        mix_dram = nc.dram_tensor("mix_scratch", [2 * KB, P, S], F32).ap()
        c8_dram = nc.dram_tensor("c8_scratch", [HEADS, S], F32).ap()

        pj = psum("pj", [P, 2, HALF])
        ps = psum("ps", [P, 2, S])
        pt = psum("pt", [P, 4, P])
        pv = psum("pv", [P, 2, 2 * P])
        pv_bank = pv[:].rearrange("p a (b c) -> p (a b) c", c=P)
        ps_bank = ps[:].rearrange("p a (b c) -> p (a b) c", c=HALF)

        g_in = sem("g_in")
        small_in = sem("small_in")
        x_in = [sem(f"x_in{i}") for i in range(TB)]
        raw_in = [sem("raw_in0"), sem("raw_in1")]
        wp_in = sem("wp_in")
        cb_in = [sem("cb_in0"), sem("cb_in1")]
        c8_stored = sem("c8_stored")
        gate_stored = [sem("gate_stored0"), sem("gate_stored1")]
        mix_in = [sem("mix_in0"), sem("mix_in1")]
        xr_in = [sem("xr_in0"), sem("xr_in1")]
        p_in = sem("p_in")
        pe_in = [sem("pe_in0"), sem("pe_in1")]
        out_stored = [sem("out_stored0"), sem("out_stored1")]
        consts = sem("consts")
        eps_set = sem("eps_set")
        ssq_done = sem("ssq_done")
        rms_done = sem("rms_done")
        rinv_done = sem("rinv_done")
        xs_done = sem("xs_done")
        xt_ready = sem("xt_ready")
        xt_hi = sem("xt_hi")
        xt_lo = sem("xt_lo")
        w_hi_done = sem("w_hi_done")
        w_lo_done = sem("w_lo_done")
        wp_hi = sem("wp_hi")
        wp_lo = sem("wp_lo")
        pj_ready = sem("pj_ready")
        pj_hi = sem("pj_hi")
        pj_free = sem("pj_free")
        z_exp = sem("z_exp")
        z_steps = sem("z_steps")
        f_steps = sem("f_steps")
        f_act = sem("f_act")
        c8_ready = sem("c8_ready")
        pool_steps = sem("pool_steps")
        pooled = sem("pooled")
        lin_ready = sem("lin_ready")
        lin_gated = sem("lin_gated")
        s_ready = sem("s_ready")
        s_shifted = sem("s_shifted")
        e_done = sem("e_done")
        rden_done = sem("rden_done")
        p_ready = sem("p_ready")
        t_ready = sem("t_ready")
        t_hi = sem("t_hi")
        t_lo = sem("t_lo")
        pv_ready = sem("pv_ready")
        pv_copied = sem("pv_copied")
        pv_added = sem("pv_added")
        attn_gated = sem("attn_gated")
        mix_hi = sem("mix_hi")
        mix_lo_pool = sem("mix_lo_pool")
        mix_lo_attn = sem("mix_lo_attn")
        o_ready = sem("o_ready")
        o_e0_used = sem("o_e0_used")
        o_evac = sem("o_evac")
        sq_used = sem("sq_used")
        ssum_ready = sem("ssum_ready")
        rr_done = sem("rr_done")
        rr_inv = sem("rr_inv")
        xr_t = sem("xr_t")
        xr_done = sem("xr_done")
        p_t = sem("p_t")
        p_hi = sem("p_hi")
        p_lo = sem("p_lo")
        h_scaled = sem("h_scaled")
        h_added = sem("h_added")
        h_hi = sem("h_hi")
        h_lo = sem("h_lo")
        pe_hi = sem("pe_hi")
        pe_lo = sem("pe_lo")
        gp_ready = sem("gp_ready")
        sig_done = sem("sig_done")
        gp_mul = sem("gp_mul")
        oT_done = sem("oT_done")
        oT_t = sem("oT_t")
        ost_done = sem("ost_done")


        stage = (vT[:], gate[:, 0])

        def f32(t):
            return t.bitcast(F32)

        def half(h):
            return slice(h * HALF, (h + 1) * HALF)

        def chunk_col(job, c, pool):
            if pool:
                return job * 256 + ((COL_U if c < 2 else COL_ZP) + P * (c % 2))
            return job * P + (COL_Z, COL_Q, COL_K, COL_V)[c]

        block = ctx.enter_context(nc.Block())

        @block.sync
        def _(sp):
            def load_w(slot, src, split):
                if split is not None:
                    sp.wait_ge(w_lo_done, split)
                sp.dma_start(w_raw[:, slot], src.rearrange("(k p) c -> p k c", p=P)).then_inc(raw_in[slot], 16)

            def load_in(job, c, pool):
                m = (job if pool else job + GROUPS) * 4 + (1 + c)
                split = m - 1 if pool else None if c == 1 else m if c == 0 else m - 1
                load_w((1 + c) % 2, w_in[0, :, bass.ds(chunk_col(job, c, pool), P)], split)

            def load_out(db, e):
                load_w((1 + e) % 2, w_out[0, (1 - e) * D:(2 - e) * D, bass.ds(db * P, P)],
                       None if e else db * 2 + CHUNK_OUT)

            def load_pg(db, par):
                load_w((1 + par) % 2, w_pg[0, :, bass.ds(db * P, P)], db + (CHUNK_PG - 1))

            sp.dma_start(x_all[:, 0], x[0, 0:P]).then_inc(x_in[0], 16)
            sp.dma_start(g_pre, norm_pre[0:1, :].broadcast_to([P, D])).then_inc(g_in, 16)
            for i in range(1, TB):
                sp.dma_start(x_all[:, i], x[0, i * P:(i + 1) * P]).then_inc(x_in[i], 16)
            load_w(0, w_in[0, :, COL_F:COL_F + P], None)
            load_w(1, w_in[0, :, COL_U:COL_U + P], None)
            with nc.allow_non_contiguous_dma(reason="a few KB of vectors"):
                sp.dma_start(bf_sb[:], b_f.rearrange("a h -> h a")).then_inc(small_in, 16)
                sp.dma_start(ramp_sb[:], ramp).then_inc(small_in, 16)
                sp.dma_start(pscale[:], pool_scale[0].rearrange("(k p) -> p k", p=P)).then_inc(small_in, 16)
                sp.dma_start(gpost[:], norm_post[0].rearrange("(k p) -> p k", p=P)).then_inc(small_in, 16)

            def load_wp(g):
                sp.dma_start(wp_raw, w_pool[0, bass.ds(g, 1)].rearrange("g (c p) n -> p (g c) n", p=P)).then_inc(wp_in, 16)

            def store_pool(g):
                for dc in range(2):
                    sp.wait_ge(lin_gated, g * 4 + (2 * dc + 2))
                    sp.dma_start(mix_dram[bass.ds(g * 2 + (KB + dc), 1)].rearrange("a p s -> (a p) s"),
                                 gate[:, dc]).then_inc(gate_stored[dc], 16)

            load_wp(0)
            load_in(0, 1, True)
            load_in(0, 2, True)
            load_in(0, 3, True)
            sp.wait_ge(c8_ready, 1)
            sp.dma_start(c8_dram, vT[0:HEADS, :]).then_inc(c8_stored, 16)
            load_in(1, 0, True)
            load_in(1, 1, True)

            def pool_loads(g, last):
                sp.wait_ge(wp_lo, g)
                load_wp(g)
                store_pool(g - 1)
                load_in(g, 2, True)
                load_in(g, 3, True)
                for c in range(2):
                    load_in(0 if last else g + 1, c, not last)

            with sp.Fori(1, GROUPS - 1) as g:
                pool_loads(g, False)
            pool_loads(GROUPS - 1, True)
            store_pool(GROUPS - 1)
            load_in(0, 2, False)
            load_in(0, 3, False)

            def load_cb(pair, hd):
                sp.dma_start(cb[:, hd], c8_dram[bass.ds(pair * 2 + hd, 1), :].broadcast_to([P, S]))\
                  .then_inc(cb_in[hd], 16)

            sp.wait_ge(c8_stored, 16)
            sp.wait_ge(xs_done, TB)
            load_cb(0, 0)
            sp.wait_ge(wp_lo, GROUPS)
            load_cb(0, 1)
            load_in(1, 0, False)
            load_in(1, 1, False)

            def pair_loads(pair, par, last):
                load_in(pair + 1, 2, False)
                load_in(pair + 1, 3, False)
                sp.wait_ge(s_shifted, pair * TILES + TB)
                load_cb(pair + 1, 0)
                for c in range(2):
                    load_out(0, c) if last else load_in(pair + 2, c, False)
                sp.wait_ge(s_shifted, pair * TILES + TILES)
                load_cb(pair + 1, 1)
                sp.wait_ge(attn_gated, pair * 8 + 8)
                sp.dma_start(mix_dram[bass.ds(pair, 1)].rearrange("a p s -> (a p) s"), gate[:, par])\
                  .then_inc(gate_stored[par], 16)

            with sp.Fori(0, 3) as a:
                pair_loads(a * 2, 0, False)
                pair_loads(a * 2 + 1, 1, False)
            pair_loads(PAIRS - 2, 0, True)
            load_out(1, 0)
            load_out(1, 1)
            sp.wait_ge(gate_stored[0], 16 * (GROUPS + 4))
            sp.wait_ge(gate_stored[1], 16 * (GROUPS + 3))
            sp.wait_ge(t_lo, NQUADS * (PAIRS - 1) + 2)
            for y in range(2 * KB - 1):
                if 2 <= y < KB:
                    sp.wait_ge(mix_lo_pool, y - 1)
                if y == KB:
                    sp.wait_ge(mix_lo_pool, KB)
                if y >= KB + 2:
                    sp.wait_ge(mix_lo_attn, y - KB - 1)
                sp.dma_start(stage[y % 2], mix_dram[(y + KB) % (2 * KB)]).then_inc(mix_in[y % 2], 16)
            with sp.Fori(1, KB - 1) as db:
                load_out(db + 1, 0)
                load_out(db + 1, 1)
            load_pg(0, 0)
            load_pg(1, 1)
            sp.wait_ge(o_ready, 2 * KB)

            def load_p(i):
                sp.dma_start(p_raw[:], p[0, 0, i * HALF:(i + 1) * HALF].rearrange("(b t) c -> t b c", t=P)).then_inc(p_in, 16)

            def load_pe(db, par):
                sp.dma_start(pe_raw[:, par], w_pe[0, :, bass.ds(db * P, P)].rearrange("(k p) c -> p k c", p=P))\
                  .then_inc(pe_in[par], 16)

            for i in range(TB):
                if i >= 2:
                    sp.wait_ge(xr_t, 2 * i - 2)
                sp.dma_start(x_raw[:, i % 2], x[0, i * P:(i + 1) * P]).then_inc(xr_in[i % 2], 16)
                if i == 1:
                    load_p(0)
                    load_pe(0, 0)
                    load_pe(1, 1)
            sp.wait_ge(p_t, 2)
            load_p(1)

            def store_out(db, h):
                sp.wait_ge(ost_done, db * 2 + (h + 1))
                sp.dma_start(out[0, half(h), bass.ds(db * P, P)].rearrange("(b t) c -> t b c", t=P),
                             gate[:, 1, half(h)].rearrange("p (b c) -> p b c", c=P)).then_inc(out_stored[h], 16)

            with sp.Fori(0, KB // 2 - 1) as a:
                for par in range(2):
                    load_pg(a * 2 + (2 + par), par)
                    sp.wait_ge(pe_lo, a * 2 + (1 + par))
                    load_pe(a * 2 + (2 + par), par)
                    store_out(a * 2 + par, 0)
                    store_out(a * 2 + par, 1)
            for db in range(KB - 2, KB):
                store_out(db, 0)
                store_out(db, 1)
            sp.wait_ge(out_stored[0], 16 * KB)
            sp.wait_ge(out_stored[1], 16 * KB)

        @block.tensor
        def _(pe):
            def three(bank, a_h, a_l, b_h, b_l, start, stop, done=None):
                pe.matmul(bank, a_h, b_h, start=start, stop=False)
                pe.matmul(bank, a_h, b_l, start=False, stop=False)
                last = pe.matmul(bank, a_l, b_h, start=False, stop=stop)
                if done is not None:
                    last.then_inc(done, 1)

            def project(slot, h, k0, k1):
                for k in range(k0, k1):
                    three(pj[:, h], w_h[:, slot, k], w_l[:, slot, k], hn_h[:, k, half(h)], hn_l[:, k, half(h)],
                          k == 0, k == KB - 1, pj_ready if k == KB - 1 else None)

            def piece(job, c, h, k0, k1):
                if k0 == 0:
                    if h == 0:
                        pe.wait_ge(w_lo_done, job * 4 + (c + 2))
                    pe.wait_ge(pj_free, job * 8 + (2 * c + h + 1))
                project((1 + c) % 2, h, k0, k1)

            def transpose_quad(dst, blocks):
                for n, b in enumerate(blocks):
                    last = pe.transpose(dst[:, n, :], b, ident[:])
                return last

            pe.wait_ge(consts, 7)
            for i in range(TB):
                pe.wait_ge(xs_done, i + 1)
                for q in range(2):
                    r = 2 * i + q
                    if r >= 4:
                        pe.wait_ge(xt_lo, r - 3)
                    transpose_quad(ps_bank[:, r % 4].rearrange("p (b t) -> p b t", t=P),
                                   [x_all[:, i, (4 * q + b) * P:(4 * q + b + 1) * P] for b in range(4)])\
                        .then_inc(xt_ready, 1)
            pe.wait_ge(w_lo_done, 1)
            for h in range(2):
                pe.wait_ge(xt_lo, TB * (h + 1))
                project(0, h, 0, KB)

            def linear(g):
                pe.wait_ge(pooled, g * 2 + 2)
                pe.wait_ge(wp_lo, g + 1)
                for dc in range(2):
                    for h in range(2):
                        for c in range(2):
                            three(ps_bank[:, 2 * dc + h], wp_h[:, c, dc * P:(dc + 1) * P], wp_l[:, c, dc * P:(dc + 1) * P],
                                  pooled_h[:, c, half(h)], pooled_l[:, c, half(h)], c == 0, c == 1, lin_ready if c else None)

            def job(j):
                for c in range(4):
                    for h in range(2):
                        piece(j, c, h, 0, KB)

            job(0)
            with pe.Fori(1, GROUPS) as g:
                linear(g - 1)
                job(g)
            linear(GROUPS - 1)
            job(GROUPS)
            pe.wait_ge(lin_gated, 4 * GROUPS)

            def scores(pair, par, n):
                hd, i = divmod(n, TB)
                rows = slice(DH * hd, DH * hd + DH)
                t = slice(i * P, (i + 1) * P)
                if n >= 2:
                    pe.wait_ge(s_shifted, pair * TILES + (n - 1))
                width = (i + 1) * P
                for c0 in range(0, width, HALF):
                    c1 = min(c0 + HALF, width)
                    diagonal = c1 == width
                    three(ps[:, n % 2, c0:c1], q_h[rows, par, t], q_l[rows, par, t], k_h[rows, par, c0:c1],
                          k_l[rows, par, c0:c1], True, not diagonal)
                    if diagonal:
                        pe.matmul(ps[:, n % 2, c1 - P:c1], ident_b[:], mask_b[:], start=False, stop=True)\
                          .then_inc(s_ready, 1)

            def turn(pair, n, q):
                at_ = pair * NQUADS + QUADS[(n, q)]
                pe.wait_ge(p_ready, pair * TILES + (n + 1))
                pe.wait_ge(t_lo, at_)
                transpose_quad(pt, [e_sb[:, n % 3, b * P:(b + 1) * P] for b in quad_blocks(n, q)]).then_inc(t_ready, 1)

            def turn_v(pair, q):
                if q == 0:
                    pe.wait_ge(pj_free, pair * 8 + (2 + 8 * GROUPS + 8))
                else:
                    pe.wait_ge(t_lo, pair * NQUADS + q)
                transpose_quad(pt, [vT[:, b * P:(b + 1) * P] for b in range(4 * q, 4 * q + 4)]).then_inc(t_ready, 1)

            def values(pair, G):
                hd, g = divmod(G, TB // 2)
                last_quad = QUADS[(2 * G + 1, 1 if 2 * g + 1 >= 4 else 0)]
                pe.wait_ge(t_lo, pair * NQUADS + (last_quad + 1))
                if G >= 2:
                    pe.wait_ge(pv_added, pair * 8 + (G - 1))
                top = 2 * g + 1
                for b in range(top + 1):
                    c0 = P if b == top else 0
                    pe.matmul(pv[:, G % 2, c0:], v_s[:, b, hd], pt_h[G % 2][:, b, c0:], start=(b == 0), stop=False)
                    last = pe.matmul(pv[:, G % 2, c0:], v_s[:, b, hd], pt_l[G % 2][:, b, c0:], start=False, stop=(b == top))
                last.then_inc(pv_ready, 1)

            def mix_piece(y):
                pe.wait_ge(mix_lo_pool, y + 1)
                if y == 0:
                    pe.wait_ge(w_lo_done, CHUNK_OUT + 1)
                    pe.wait_ge(pj_free, HALF_OUT)
                for h in range(2):
                    three(pj[:, h], w_h[:, 1, y], w_l[:, 1, y], hn_h[:, y, half(h)], hn_l[:, y, half(h)], y == 0, False,
                          o_e0_used if (y, h) == (KB - 1, 1) else None)

            def attend(pair, par, last=False):
                for n in range(STEPS):
                    fill = [] if last else [(c, h, k0) for c, h, k0 in pieces(n)]

                    def filler():
                        if fill:
                            c, h, k0 = fill.pop(0)
                            piece(pair + (GROUPS + 1), c, h, k0, k0 + 2)
                    if n < TILES:
                        if n == 0:
                            pe.wait_ge(pj_free, pair * 8 + (2 + 8 * GROUPS + 6))
                        scores(pair, par, n)
                    filler()
                    if n < 2:
                        turn_v(pair, n)
                    if 2 <= n < TILES + 2:
                        turn(pair, n - 2, 0)
                    filler()
                    if (n - 2, 1) in QUADS:
                        turn(pair, n - 2, 1)
                    filler()
                    if last and n >= 3 and n % 2:
                        mix_piece((n - 3) // 2)
                    if n >= 4 and n % 2 == 0:
                        values(pair, (n - 4) // 2)

            with pe.Fori(0, 3) as a:
                attend(a * 2, 0)
                attend(a * 2 + 1, 1)
            attend(PAIRS - 2, 0)
            attend(PAIRS - 1, 1, True)

            def out_half(h, e, waits=False):
                slot, m_h, m_l = ((1, hn_h, hn_l), (0, at_h, at_l))[e]
                for k in range(KB):
                    if waits:
                        pe.wait_ge(mix_lo_attn, k + 1)
                    done = o_ready if e else o_e0_used if h else None
                    three(pj[:, h], w_h[:, slot, k], w_l[:, slot, k], m_h[:, k, half(h)], m_l[:, k, half(h)],
                          e == 0 and k == 0, e == 1 and k == KB - 1, done if k == KB - 1 else None)

            pe.wait_ge(w_lo_done, CHUNK_OUT + 2)
            out_half(0, 1, True)
            out_half(1, 1)
            with pe.Fori(1, KB) as db:
                pe.wait_ge(w_lo_done, db * 2 + (CHUNK_OUT + 1))
                for h in range(2):
                    pe.wait_ge(o_evac, db * 2 + (h - 1))
                    out_half(h, 0)
                pe.wait_ge(w_lo_done, db * 2 + (CHUNK_OUT + 2))
                for h in range(2):
                    out_half(h, 1)
            for h in range(2):
                pe.wait_ge(sq_used, 2 * KB - 1 + h)
                pe.matmul(ps_bank[:, h], ones[:], gate[:, 1, half(h)], start=True, stop=True).then_inc(ssum_ready, 1)

            def turn_p(r):
                hh, kk = divmod(r, 2)
                pe.wait_ge(p_in, 16 * (hh + 1))
                if r >= 2:
                    pe.wait_ge(p_lo, r - 1)
                transpose_quad((pt[:], pv_bank)[r % 2], [p_raw[:, b, kk * P:(kk + 1) * P] for b in range(4)]).then_inc(p_t, 1)

            for i in range(TB):
                pe.wait_ge(xr_in[i % 2], 16 * (i // 2 + 1))
                for q in range(2):
                    r = 2 * i + q
                    if r >= 2:
                        pe.wait_ge(xr_done, r - 1)
                    transpose_quad(ps_bank[:, 2 + r % 2].rearrange("p (b t) -> p b t", t=P),
                                   [x_raw[:, i % 2, (4 * q + b) * P:(4 * q + b + 1) * P] for b in range(4)])\
                        .then_inc(xr_t, 1)
                if i == 2:
                    turn_p(0)
                    turn_p(1)
            turn_p(2)
            turn_p(3)

            def gate_half(db, par, h, first=False):
                slot = (1 + par) % 2
                if h == 0:
                    pe.wait_ge(w_lo_done, db + (CHUNK_PG + 1))
                if not first:
                    pe.wait_ge(sig_done, db * 2 + (h - 1))
                for k in range(KB):
                    if first and h == 0:
                        pe.wait_ge(h_lo, k + 1)
                    three(pj[:, h], w_h[:, slot, k], w_l[:, slot, k], hn_h[:, k, half(h)], hn_l[:, k, half(h)],
                          k == 0, k == KB - 1)
                pe.wait_ge(pe_lo, db + 1)
                if first:
                    pe.wait_ge(p_lo, 4)
                else:
                    pe.wait_ge(gp_mul, db * 2 + (h - 1))
                for k in range(PB):
                    three(ps_bank[:, h], pe_h[:, par, k], pe_l[:, par, k], pT_h[:, k, half(h)], pT_l[:, k, half(h)],
                          k == 0, k == PB - 1, gp_ready if k == PB - 1 else None)

            def turn_out(db, h, first=False):
                pe.wait_ge(oT_done, db * 2 + (h + 1))
                if not first:
                    pe.wait_ge(ost_done, db * 2 + (h - 1))
                transpose_quad((pt[:], pv_bank)[h], [gate[:, 0, h * HALF + b * P:h * HALF + (b + 1) * P] for b in range(4)])\
                    .then_inc(oT_t, 1)

            def gate_block(db, par):
                gate_half(db, par, 0)
                turn_out(db - 1, 1)
                gate_half(db, par, 1)
                turn_out(db, 0)

            gate_half(0, 0, 0, True)
            gate_half(0, 0, 1, True)
            turn_out(0, 0, True)
            gate_half(1, 1, 0)
            turn_out(0, 1, True)
            gate_half(1, 1, 1)
            turn_out(1, 0)
            with pe.Fori(1, KB // 2) as a:
                gate_block(a * 2, 0)
                gate_block(a * 2 + 1, 1)
            turn_out(KB - 1, 1)

        @block.scalar
        def _(act):
            def split_hi(slot, loads):
                act.wait_ge(raw_in[slot], loads * 16)
                act.activation(w_h[:, slot], w_raw[:, slot], ACT.Copy).then_inc(w_hi_done, 1)

            def split_next(job, c):
                act.wait_ge(pj_ready, job * 8 + (2 * c + 2))
                split_hi(c % 2, job * 2 + (c // 2 + 2))

            def split_out(db, e):
                act.wait_ge(o_ready if e else o_e0_used, db * 2 if e else db)
                split_hi((1 + e) % 2, db + (CHUNK_OUT // 2 + 1 + e))

            def x_quads(i):
                for q in range(2):
                    r = 2 * i + q
                    act.wait_ge(xt_ready, r + 1)
                    act.activation(hn_h[:, 4 * q:4 * q + 4, i * P:(i + 1) * P],
                                   ps_bank[:, r % 4].rearrange("p (b t) -> p b t", t=P), ACT.Copy).then_inc(xt_hi, 1)

            act.wait_ge(eps_set, 1)
            for i in range(TB):
                act.wait_ge(x_in[i], 16)
                act.activation(vT[:], x_all[:, i], ACT.Square, accum_out=ssq[:, i:i + 1]).then_inc(ssq_done, 1)
                act.wait_ge(ssq_done, i + 1)
                act.activation(rms[:, i:i + 1], ssq[:, i:i + 1], ACT.Sqrt, bias=eps_sb[:], scale=1.0 / D).then_inc(rms_done, 1)
                if i == 1:
                    split_hi(0, 1)
                if i >= 2:
                    x_quads(i - 2)
            x_quads(TB - 2)
            x_quads(TB - 1)
            split_hi(1, 1)
            act.wait_ge(pj_free, 2)
            act.activation(gate[0:HEADS, 1], gate[0:HEADS, 0], ACT.Abs).then_inc(f_act, 1)
            act.wait_ge(f_act, 1)
            act.activation(gate[0:HEADS, 1], gate[0:HEADS, 1], ACT.Exp, scale=-1.0).then_inc(f_act, 1)
            act.wait_ge(f_act, 2)
            act.activation(gate[0:HEADS, 1], gate[0:HEADS, 1], ACT.Ln, bias=1.0).then_inc(f_act, 1)

            def z_half(job, c, h, dst, index):
                act.wait_ge(pj_ready, job * 8 + (3 + 2 * c + h))
                act.activation(dst, pj[:, h], ACT.Exp, scale=-1.0).then_inc(z_exp, 1)

            def pool_job(g, first=False):
                for c in range(4):
                    split_next(g, c)
                    if c == 0:
                        act.wait_ge(wp_in, g * 16 + 16)
                        if not first:
                            act.wait_ge(lin_ready, g * 4)
                        act.activation(wp_h, wp_raw, ACT.Copy).then_inc(wp_hi, 1)
                    if c >= 2:
                        if first:
                            act.wait_ge(c8_ready, 1)
                        else:
                            act.wait_ge(gate_stored[c - 2], g * 16)
                        for h in range(2):
                            z_half(g, c, h, gate[:, c - 2, half(h)], None)

            pool_job(0, True)
            with act.Fori(1, GROUPS) as g:
                pool_job(g)

            def evacuate(pair, par, stored, c, h):
                if c == 0 and h == 0:
                    act.wait_ge(gate_stored[par], stored * 16)
                if c == 0:
                    z_half(pair + GROUPS, c, h, gate[:, par, half(h)], None)
                elif c < 3:
                    act.wait_ge(pj_ready, pair * 8 + (8 * GROUPS + 3 + 2 * c + h))
                    act.activation((q_h, k_h)[c - 1][:, par, half(h)], pj[:, h], ACT.Copy).then_inc(pj_hi, 1)

            for c in range(4):
                split_next(GROUPS, c)
                for h in range(2):
                    evacuate(0, 0, GROUPS, c, h)

            def quad_hi(pair, n, q):
                act.wait_ge(t_ready, pair * NQUADS + (QUADS[(n, q)] + 1))
                G = n // 2
                if G >= 2 and n % 2 == 0 and q == 0:
                    act.wait_ge(pv_ready, pair * 8 + (G - 1))
                bs = quad_blocks(n, q)
                act.activation(pt_h[G % 2][:, bs[0]:bs[-1] + 1, (n % 2) * P:(n % 2 + 1) * P], pt[:, 0:len(bs)], ACT.Copy)\
                   .then_inc(t_hi, 1)

            def v_hi(pair, q):
                act.wait_ge(t_ready, pair * NQUADS + (q + 1))
                act.activation(v_s[:, 4 * q:4 * q + 4, :, 0:DH], pt[:].rearrange("p b (h d) -> p b h d", h=2), ACT.Copy)\
                   .then_inc(t_hi, 1)

            def exps(pair, n):
                act.wait_ge(s_shifted, pair * TILES + (n + 1))
                e = e_sb[:, n % 3, 0:(n % TB + 1) * P]
                act.activation(e, e, ACT.Exp, bias=neg_max[:, n % 3:n % 3 + 1], scale=-1.0,
                               accum_out=den[:, n % 3:n % 3 + 1]).then_inc(e_done, 1)

            def v_copy(pair, G):
                hd = G // 4
                act.wait_ge(pv_ready, pair * 8 + (G + 1))
                if G >= 2:
                    act.wait_ge(attn_gated, pair * 8 + (G - 1))
                act.activation(pv_tmp[DH * hd:DH * hd + DH, G % 2], pv[DH * (1 - hd):DH * (1 - hd) + DH, G % 2], ACT.Copy)\
                   .then_inc(pv_copied, 1)

            def mix_part(y):
                if y < 2 * KB - 1:
                    act.wait_ge(mix_in[y % 2], 16 * (y // 2 + 1))
                else:
                    act.wait_ge(attn_gated, 8 * PAIRS)
                dst = hn_h[:, y] if y < KB else at_h[:, y - KB]
                act.activation(dst, stage[y % 2] if y < 2 * KB - 1 else gate[:, 1], ACT.Copy).then_inc(mix_hi, 1)

            def attend(pair, nxt, par, stored, last=False):
                for n in range(STEPS):
                    fill = [] if last else pieces(n)
                    for c, h, k0 in fill:
                        if (h, k0) == (0, 0):
                            split_next(pair + (GROUPS + 1), c)
                    if last and n == 0:
                        act.wait_ge(pj_ready, HALF_OUT)
                        split_hi(0, CHUNK_OUT // 2 + 2)
                    if n < 2:
                        v_hi(pair, n)
                    if 2 <= n < TILES + 2:
                        quad_hi(pair, n - 2, 0)
                    if n < TILES:
                        exps(pair, n)
                    if (n - 2, 1) in QUADS:
                        quad_hi(pair, n - 2, 1)
                    for c, h, k0 in fill:
                        if k0 == KB - 2:
                            evacuate(nxt, 1 - par, stored, c, h)
                    if last and 2 <= n < TILES + 2 and n % 2 == 0:
                        mix_part((n - 2) // 2)
                    if n >= 4 and n % 2 == 0:
                        v_copy(pair, (n - 4) // 2)

            with act.Fori(0, 3) as a:
                attend(a * 2, a * 2 + 1, 0, a + GROUPS)
                attend(a * 2 + 1, a * 2 + 2, 1, a + (GROUPS + 1))
            attend(PAIRS - 2, PAIRS - 1, 0, 3 + GROUPS)
            attend(PAIRS - 1, None, 1, None, True)

            for y in range(KB, 2 * KB):
                mix_part(y)
                if y == KB + 4:
                    split_out(1, 0)

            def out_evac(db, first=False):
                for h in range(2):
                    act.wait_ge(o_ready, db * 2 + (h + 1))
                    act.activation(mixed[:, bass.ds(db, 1), half(h)].rearrange("p a s -> p (a s)"), pj[:, h], ACT.Copy)
                    if not first:
                        act.wait_ge(sq_used, db * 2 + (h - 1))
                    act.activation(vT[:, half(h)], pj[:, h], ACT.Square).then_inc(o_evac, 1)

            out_evac(0, True)
            split_out(1, 1)
            split_out(2, 0)
            with act.Fori(1, KB - 2) as db:
                out_evac(db)
                split_out(db + 1, 1)
                split_out(db + 2, 0)
            out_evac(KB - 2)
            split_out(KB - 1, 1)

            def split_pg(par, loads):
                split_hi((1 + par) % 2, loads)

            act.wait_ge(o_e0_used, KB)
            split_pg(0, CHUNK_PG // 2 + 1)
            out_evac(KB - 1)
            for h in range(2):
                act.wait_ge(ssum_ready, h + 1)
                act.activation(vT[:, half(h)], ps_bank[:, h], ACT.Sqrt, bias=eps_sb[:], scale=1.0 / D).then_inc(rr_done, 1)
            split_pg(1, CHUNK_PG // 2 + 2)

            def p_part(r):
                hh, kk = divmod(r, 2)
                act.wait_ge(p_t, r + 1)
                act.activation(pT_h[:, kk, half(hh)].rearrange("p (b t) -> p b t", t=P), (pt[:], pv_bank)[r % 2], ACT.Copy)\
                   .then_inc(p_hi, 1)

            def pe_part(par, loads):
                act.wait_ge(pe_in[par], loads * 16)
                act.activation(pe_h[:, par], pe_raw[:, par], ACT.Copy).then_inc(pe_hi, 1)

            for i in range(TB):
                for q in range(2):
                    r = 2 * i + q
                    act.wait_ge(xr_t, r + 1)
                    act.activation(xT[:, 4 * q:4 * q + 4, i * P:(i + 1) * P],
                                   ps_bank[:, 2 + r % 2].rearrange("p (b t) -> p b t", t=P), ACT.Copy).then_inc(xr_done, 1)
                if i == 2:
                    p_part(0)
                    p_part(1)
            p_part(2)
            p_part(3)
            pe_part(0, 1)
            pe_part(1, 1)
            for k in range(KB):
                act.wait_ge(h_added, k + 1)
                act.activation(hn_h[:, k], mixed[:, k], ACT.Copy).then_inc(h_hi, 1)

            def sigmoid(db, h, first=False):
                act.wait_ge(gp_ready, db * 2 + (h + 1))
                if not first:
                    act.wait_ge(oT_t, db * 2 + (h - 1))
                act.activation(gate[:, 0, half(h)], pj[:, h], ACT.Sigmoid).then_inc(sig_done, 1)

            def out_copy(db, h, first=False):
                act.wait_ge(oT_t, db * 2 + (h + 1))
                if not first:
                    act.wait_ge(out_stored[h], db * 16)
                act.activation(gate[:, 1, half(h)].rearrange("p (b c) -> p b c", c=P), (pt[:], pv_bank)[h], ACT.Copy)\
                   .then_inc(ost_done, 1)

            def gate_block(db, par, a, more):
                sigmoid(db, 0)
                out_copy(db - 1, 1)
                sigmoid(db, 1)
                if more:
                    split_pg(par, a + (CHUNK_PG // 2 + 2 + par))
                    pe_part(par, a + 2)
                out_copy(db, 0)

            sigmoid(0, 0, True)
            sigmoid(0, 1, True)
            split_pg(0, CHUNK_PG // 2 + 2)
            pe_part(0, 2)
            out_copy(0, 0, True)
            sigmoid(1, 0)
            out_copy(0, 1, True)
            sigmoid(1, 1)
            split_pg(1, CHUNK_PG // 2 + 3)
            pe_part(1, 2)
            out_copy(1, 0)
            with act.Fori(1, KB // 2 - 1) as a:
                gate_block(a * 2, 0, a, True)
                gate_block(a * 2 + 1, 1, a, True)
            gate_block(KB - 2, 0, None, False)
            gate_block(KB - 1, 1, None, False)
            out_copy(KB - 1, 1)

        @block.gpsimd
        def _(pool):
            pool.memset(ident[:], 0.0).then_inc(consts, 1)
            pool.memset(ident_b[:], 0.0).then_inc(consts, 1)
            pool.memset(mask_b[:], 0.0).then_inc(consts, 1)
            pool.memset(ones[:], 1.0).then_inc(consts, 1)
            pool.wait_ge(consts, 4)
            for t in (ident, ident_b):
                pool.affine_select(out=t[:], in_=t[:], compare_op=ALU.not_equal, fill=1.0, base=0,
                                   pattern=[[-1, P]], channel_multiplier=1).then_inc(consts, 1)
            pool.affine_select(out=mask_b[:], in_=mask_b[:], compare_op=ALU.is_ge, fill=MASKED, base=0,
                               pattern=[[-1, P]], channel_multiplier=1).then_inc(consts, 1)

            def lo(slot, m):
                pool.wait_ge(w_hi_done, m + 1)
                pool.tensor_tensor(w_l[:, slot], w_raw[:, slot], f32(w_h[:, slot]), ALU.subtract).then_inc(w_lo_done, 1)

            lo(0, 0)
            lo(1, 1)

            def job_lo(j, c):
                lo(c % 2, j * 4 + (c + 2))

            def pool_job(g):
                job_lo(g, 0)
                pool.wait_ge(wp_hi, g + 1)
                pool.tensor_tensor(wp_l, wp_raw, f32(wp_h), ALU.subtract).then_inc(wp_lo, 1)
                for c in range(1, 4):
                    job_lo(g, c)

            with pool.Fori(0, GROUPS) as g:
                pool_job(g)
            with pool.Fori(GROUPS, GROUPS + PAIRS) as j:
                for c in range(4):
                    job_lo(j, c)
            lo(0, CHUNK_OUT + 1)
            for y in range(KB):
                pool.wait_ge(mix_hi, y + 1)
                pool.tensor_tensor(hn_l[:, y], stage[y % 2], f32(hn_h[:, y]), ALU.subtract).then_inc(mix_lo_pool, 1)
            with pool.Fori(1, KB) as db:
                lo(1, db * 2 + CHUNK_OUT)
                lo(0, db * 2 + (CHUNK_OUT + 1))
            lo(1, CHUNK_PG)
            lo(0, CHUNK_PG + 1)

            def pe_low(par, db):
                pool.wait_ge(pe_hi, db + 1)
                pool.tensor_tensor(pe_l[:, par], pe_raw[:, par], f32(pe_h[:, par]), ALU.subtract).then_inc(pe_lo, 1)

            pe_low(0, 0)
            pe_low(1, 1)
            pool.wait_ge(xr_done, 2 * TB)
            for k in range(KB):
                pool.wait_ge(h_scaled, k + 1)
                pool.tensor_tensor(mixed[:, k], mixed[:, k], xT[:, k], ALU.add).then_inc(h_added, 1)
            with pool.Fori(0, KB // 2 - 1) as a:
                for par in range(2):
                    lo((1 + par) % 2, a * 2 + (CHUNK_PG + 2 + par))
                    pe_low(par, a * 2 + (2 + par))

        @block.vector
        def _(dve):
            def x_quads(i):
                for q in range(2):
                    r = 2 * i + q
                    dve.wait_ge(xt_hi, r + 1)
                    cols = slice(i * P, (i + 1) * P)
                    dve.tensor_tensor(hn_l[:, 4 * q:4 * q + 4, cols], ps_bank[:, r % 4].rearrange("p (b t) -> p b t", t=P),
                                      f32(hn_h[:, 4 * q:4 * q + 4, cols]), ALU.subtract).then_inc(xt_lo, 1)

            dve.memset(eps_sb[:], EPS).then_inc(eps_set, 1)
            for i in range(TB):
                dve.wait_ge(rms_done, i + 1)
                dve.reciprocal(rinv[:, i:i + 1], rms[:, i:i + 1]).then_inc(rinv_done, 1)
                dve.wait_ge(rinv_done, i + 1)
                if i == 0:
                    dve.wait_ge(g_in, 16)
                dve.scalar_tensor_tensor(out=x_all[:, i], in0=x_all[:, i], scalar=rinv[:, i:i + 1], in1=g_pre,
                                         op0=ALU.mult, op1=ALU.mult).then_inc(xs_done, 1)
                if i >= 2:
                    x_quads(i - 2)
            x_quads(TB - 2)
            x_quads(TB - 1)

            dve.wait_ge(small_in, 64)
            for h in range(2):
                dve.wait_ge(pj_ready, h + 1)
                if h == 0:
                    dve.wait_ge(ssq_done, TB)
                dve.tensor_scalar(gate[0:HEADS, 0, half(h)], pj[0:HEADS, h], bf_sb[:], -1.0, ALU.add, ALU.mult)\
                   .then_inc(pj_free, 1)
            dve.memset(e_sb[:, 1, 0:PAD], 0.0).then_inc(f_steps, 1)
            dve.wait_ge(f_act, 3)
            dve.scalar_tensor_tensor(out=gate[0:HEADS, 1], in0=gate[0:HEADS, 0], scalar=0.0, in1=gate[0:HEADS, 1],
                                     op0=ALU.max, op1=ALU.add).then_inc(f_steps, 1)
            dve.wait_ge(f_steps, 2)
            dve.wait_ge(consts, 4)
            dve.tensor_tensor_scan(vT[0:HEADS, :], ones[0:HEADS, 0:1].broadcast_to([HEADS, S]), gate[0:HEADS, 1], 0.0,
                                   ALU.mult, ALU.add).then_inc(f_steps, 1)
            dve.wait_ge(f_steps, 3)
            dve.tensor_scalar(vT[0:HEADS, :], vT[0:HEADS, :], 1.0 / SCALE, None, ALU.mult).then_inc(c8_ready, 1)

            def z_half(dst, h, index, free):
                dve.wait_ge(z_exp, index + 1)
                dve.tensor_scalar(dst, dst, 1.0, None, ALU.add).then_inc(z_steps, 1)
                dve.wait_ge(z_steps, index * 2 + 1)
                dve.reciprocal(dst, dst).then_inc(z_steps, 1)
                dve.wait_ge(z_steps, index * 2 + 2)
                dve.tensor_tensor(dst, pj[:, h], dst, ALU.mult).then_inc(pj_free, 1)

            def gate_linear(g):
                dve.wait_ge(pj_free, 8 * g + 10)
                for dc in range(2):
                    for h in range(2):
                        n = 4 * g + 2 * dc + h
                        dve.wait_ge(lin_ready, n + 1)
                        dve.scalar_tensor_tensor(out=gate[:, dc, half(h)], in0=ps_bank[:, 2 * dc + h],
                                                 scalar=pscale[:, 2 * g + dc:2 * g + dc + 1], in1=gate[:, dc, half(h)],
                                                 op0=ALU.mult, op1=ALU.mult).then_inc(lin_gated, 1)

            steps = [0]

            def then(ins):
                ins.then_inc(pool_steps, 1)
                steps[0] += 1

            def pool_window(g, c):
                w = WINDOWS[g]
                u, sums, win = e_sb[:, 0, 0:S], e_sb[:, 1], e_sb[:, 2, 0:S]
                dve.wait_ge(pj_free, 8 * g + 4 + 2 * c)
                if (g, c) == (0, 0):
                    dve.wait_ge(f_steps, 1)
                then(dve.tensor_tensor_scan(sums[:, PAD:], ones[:, 0:1].broadcast_to([P, S]), u, 0.0, ALU.mult, ALU.add))
                dve.wait_ge(pool_steps, steps[0])
                then(dve.tensor_tensor(win, sums[:, PAD:], sums[:, PAD - w:PAD - w + S], ALU.subtract))
                dve.wait_ge(pool_steps, steps[0])
                then(dve.tensor_tensor(win[:, 0:PAD], win[:, 0:PAD], ramp_sb[:, g], ALU.mult))
                dve.wait_ge(pool_steps, steps[0])
                then(dve.scalar_tensor_tensor(out=win, in0=win, scalar=1.0 / w, in1=u, op0=ALU.mult, op1=ALU.subtract))
                dve.wait_ge(pool_steps, steps[0])
                if g > 0:
                    dve.wait_ge(lin_ready, 4 * g)
                then(dve.tensor_copy(pooled_h[:, c], win))
                dve.wait_ge(pool_steps, steps[0])
                dve.tensor_tensor(pooled_l[:, c], win, f32(pooled_h[:, c]), ALU.subtract).then_inc(pooled, 1)

            for g in range(GROUPS):
                if g:
                    gate_linear(g - 1)
                for c in range(4):
                    for h in range(2):
                        if c < 2:
                            dve.wait_ge(pj_ready, 8 * g + 3 + 2 * c + h)
                            dve.tensor_copy(e_sb[:, 0, half(h)], pj[:, h]).then_inc(pj_free, 1)
                        else:
                            z_half(gate[:, c - 2, half(h)], h, 4 * g + 2 * (c - 2) + h, None)
                    if c < 2:
                        pool_window(g, c)
            gate_linear(GROUPS - 1)

            def evacuate(pair, par, c, h):
                if c == 0:
                    z_half(gate[:, par, half(h)], h, pair * 2 + (4 * GROUPS + h), None)
                elif c < 3:
                    dve.wait_ge(pj_hi, pair * 4 + (2 * c + h - 1))
                    hi, low = ((q_h, q_l), (k_h, k_l))[c - 1]
                    dve.tensor_tensor(low[:, par, half(h)], pj[:, h], f32(hi[:, par, half(h)]), ALU.subtract)\
                       .then_inc(pj_free, 1)
                else:
                    dve.wait_ge(pj_ready, pair * 8 + (8 * GROUPS + 9 + h))
                    dve.tensor_copy(vT[:, half(h)], pj[:, h]).then_inc(pj_free, 1)

            dve.wait_ge(c8_stored, 16)
            for c in range(4):
                for h in range(2):
                    evacuate(0, 0, c, h)

            def wait_scores(pair, n):
                if n % TB == 0:
                    dve.wait_ge(cb_in[n // TB], pair * 16 + 16)
                dve.wait_ge(s_ready, pair * TILES + (n + 1))

            def shift(pair, n):
                hd, w = n // TB, (n % TB + 1) * P
                dve.tensor_tensor_reduce(e_sb[:, n % 3, 0:w], ps[:, n % 2, 0:w], cb[:, hd, 0:w], -SCALE, 3e38,
                                         ALU.add, ALU.min, neg_max[:, n % 3:n % 3 + 1]).then_inc(s_shifted, 1)

            def normalise(pair, n):
                s = slice(n % 3, n % 3 + 1)
                e = e_sb[:, n % 3, 0:(n % TB + 1) * P]
                if n + 1 < TILES:
                    wait_scores(pair, n + 1)
                dve.wait_ge(e_done, pair * TILES + (n + 1))
                dve.reciprocal(rden[:, s], den[:, s]).then_inc(rden_done, 1)
                dve.wait_ge(rden_done, pair * TILES + (n + 1))
                dve.tensor_scalar(e, e, rden[:, s], None, ALU.mult).then_inc(p_ready, 1)

            def quad_lo(pair, n, q):
                G, bs = n // 2, quad_blocks(n, q)
                at_ = (slice(None), slice(bs[0], bs[-1] + 1), slice((n % 2) * P, (n % 2 + 1) * P))
                dve.wait_ge(t_hi, pair * NQUADS + (QUADS[(n, q)] + 1))
                dve.tensor_tensor(pt_l[G % 2][at_], pt[:, 0:len(bs)], f32(pt_h[G % 2][at_]), ALU.subtract)\
                   .then_inc(t_lo, 1)

            def v_lo(pair, q):
                dve.wait_ge(t_hi, pair * NQUADS + (q + 1))
                dve.tensor_tensor(v_s[:, 4 * q:4 * q + 4, :, DH:P], pt[:].rearrange("p b (h d) -> p b h d", h=2),
                                  f32(v_s[:, 4 * q:4 * q + 4, :, 0:DH]), ALU.subtract).then_inc(t_lo, 1)

            def add_and_gate(pair, par, G):
                hd = G // 4
                rows = slice(DH * hd, DH * hd + DH)
                cols = slice((G % 4) * 2 * P, (G % 4 + 1) * 2 * P)
                dve.wait_ge(pv_copied, pair * 8 + (G + 1))
                dve.tensor_tensor(pv_tmp[rows, G % 2], pv[rows, G % 2], pv_tmp[rows, G % 2], ALU.add).then_inc(pv_added, 1)
                dve.wait_ge(pv_added, pair * 8 + (G + 1))
                dve.tensor_tensor(gate[rows, par, cols], gate[rows, par, cols], pv_tmp[rows, G % 2], ALU.mult)\
                   .then_inc(attn_gated, 1)

            def attend(pair, nxt, par, last=False):
                for n in range(STEPS):
                    if n == 0:
                        wait_scores(pair, 0)
                        dve.memset(wait_sb[:], 0.0)
                    if 1 <= n <= TILES:
                        normalise(pair, n - 1)
                    if n < TILES:
                        shift(pair, n)
                    if n < 2:
                        v_lo(pair, n)
                    for q in range(2):
                        if (n - 2, q) in QUADS:
                            quad_lo(pair, n - 2, q)
                    if n >= 4 and n % 2 == 0:
                        add_and_gate(pair, par, (n - 4) // 2)
                    for c, h, k0 in [] if last else pieces(n):
                        if k0 == KB - 2:
                            evacuate(nxt, 1 - par, c, h)

            with dve.Fori(0, 3) as a:
                attend(a * 2, a * 2 + 1, 0)
                attend(a * 2 + 1, a * 2 + 2, 1)
            attend(PAIRS - 2, PAIRS - 1, 0)
            attend(PAIRS - 1, None, 1, True)

            for k in range(KB):
                dve.wait_ge(mix_hi, KB + k + 1)
                src = stage[k % 2] if k < KB - 1 else gate[:, 1]
                dve.tensor_tensor(at_l[:, k], src, f32(at_h[:, k]), ALU.subtract).then_inc(mix_lo_attn, 1)

            for h in range(2):
                dve.wait_ge(o_evac, h + 1)
                dve.tensor_copy(gate[:, 1, half(h)], vT[:, half(h)]).then_inc(sq_used, 1)
            with dve.Fori(1, KB) as db:
                for h in range(2):
                    dve.wait_ge(o_evac, db * 2 + (h + 1))
                    dve.wait_ge(sq_used, db * 2 + (h - 1))
                    dve.tensor_tensor(gate[:, 1, half(h)], gate[:, 1, half(h)], vT[:, half(h)], ALU.add)\
                       .then_inc(sq_used, 1)
            for h in range(2):
                dve.wait_ge(rr_done, h + 1)
                dve.reciprocal(vT[:, half(h)], vT[:, half(h)]).then_inc(rr_inv, 1)

            def scale(k):
                dve.scalar_tensor_tensor(out=mixed[:, k], in0=mixed[:, k], scalar=gpost[:, k:k + 1], in1=vT[:],
                                         op0=ALU.mult, op1=ALU.mult).then_inc(h_scaled, 1)

            def h_low(k):
                dve.wait_ge(h_hi, k + 1)
                dve.tensor_tensor(hn_l[:, k], mixed[:, k], f32(hn_h[:, k]), ALU.subtract).then_inc(h_lo, 1)

            def p_low(r):
                hh, kk = divmod(r, 2)
                dve.wait_ge(p_hi, r + 1)
                dve.tensor_tensor(pT_l[:, kk, half(hh)].rearrange("p (b t) -> p b t", t=P), (pt[:], pv_bank)[r % 2],
                                  f32(pT_h[:, kk, half(hh)]).rearrange("p (b t) -> p b t", t=P), ALU.subtract)\
                   .then_inc(p_lo, 1)

            p_low(0)
            p_low(1)
            dve.wait_ge(rr_inv, 2)
            scale(0)
            scale(1)
            p_low(2)
            p_low(3)
            for k in range(2, KB):
                scale(k)
                h_low(k - 2)
            h_low(KB - 2)
            h_low(KB - 1)

            def finish(db, h):
                g = gate[:, 0, half(h)]
                dve.wait_ge(sig_done, db * 2 + (h + 1))
                dve.tensor_tensor(g, ps_bank[:, h], g, ALU.mult).then_inc(gp_mul, 1)
                dve.wait_ge(gp_mul, db * 2 + (h + 1))
                dve.tensor_tensor(g, g, mixed[:, bass.ds(db, 1), half(h)].rearrange("p a s -> p (a s)"), ALU.add)\
                   .then_inc(oT_done, 1)

            with dve.Fori(0, KB) as db:
                finish(db, 0)
                finish(db, 1)


_INS = ["x", "p", "norm_pre", "norm_post", "w_in", "b_f", "w_pool", "pool_scale", "w_out", "w_pg", "w_pe"]


def kernel(**inputs):
    import numpy as np
    import concourse.bacc as bacc
    from concourse import mybir as mb
    from concourse.bass_utils import run_bass_kernel_spmd

    nc = bacc.Bacc("TRN2", target_bir_lowering=False, num_devices=1)
    arrays, args = {}, []
    for name in _INS:
        a = np.ascontiguousarray(inputs[name])
        arrays[f"in_{name}"] = a
        args.append(nc.dram_tensor(f"in_{name}", a.shape, mb.dt.from_np(a.dtype), kind="ExternalInput").ap())
    ramp = np.ones((128, 4, 16), np.float32)
    for g, w in enumerate((2, 4, 8, 16)):
        ramp[:, g, :w] = np.float32(w) / np.arange(1, w + 1, dtype=np.float32)
    arrays["in_ramp"] = ramp
    args.append(nc.dram_tensor("in_ramp", ramp.shape, mb.dt.float32, kind="ExternalInput").ap())
    args.append(nc.dram_tensor("out_0", (1, 1024, 1024), mb.dt.float32, kind="ExternalOutput").ap())
    hymba_kernel(nc, *args)
    r = run_bass_kernel_spmd(nc, [arrays], core_ids=[0])
    return r.results[0]["out_0"]
```

```python
from contextlib import ExitStack

import concourse.bass as bass
from concourse import mybir

F32 = mybir.dt.float32
F32R = mybir.dt.float32r
BF16 = mybir.dt.bfloat16
ACT = mybir.ActivationFunctionType
ALU = mybir.AluOpType

P = 128
D = 1024
S = 1024
KB = D // P
TB = S // P
HALF = 512
HEADS = 16
DH = 64
PAIRS = HEADS // 2
WINDOWS = (2, 4, 8, 16)
GROUPS = len(WINDOWS)
PAD = max(WINDOWS)
PLE = 256
PB = PLE // P
EPS = 1e-6
SCALE = DH ** -0.5
MASKED = -1e30

COL_Q, COL_K, COL_V, COL_Z = 0, D, 2 * D, 3 * D
COL_F = 4 * D
COL_U = COL_F + HEADS
COL_ZP = COL_U + D

JOB_PAIR = GROUPS
JOB_OUT_POOL = JOB_PAIR + PAIRS
JOB_OUT_ATTN = JOB_OUT_POOL + KB // 4
JOB_PG = JOB_OUT_ATTN + KB // 4


def first_half(job):
    return 2 + 8 * job


TILES = 2 * TB
STEPS = TILES + 3
QUADS = {}
for _n in range(TILES):
    for _q in range(1 if _n % TB < 4 else 2):
        QUADS[(_n, _q)] = 2 + len(QUADS)
NQUADS = 2 + len(QUADS)
PLAN = [2, 2, 1, 1, 1, 1, 2, 2, 2, 2, 1, 2, 1, 1, 2, 2, 2, 2, 3]
PLAN_EARLY = [3, 2, 2, 2, 1, 1, 2, 2, 2, 2, 2, 2, 2, 2, 2, 2, 1, 0, 0]
PLAN_LATE = [0, 1, 1, 1, 1, 2, 2, 2, 2, 2, 2, 2, 2, 2, 2, 2, 2, 2, 2]
for _plan in (PLAN, PLAN_EARLY, PLAN_LATE):
    assert len(_plan) == STEPS and sum(_plan) == 4 * 2 * (KB // 2)


def pieces(plan, n):
    at = sum(plan[:n])
    return [(i // 8, i // 4 % 2, 2 * (i % 4)) for i in range(at, at + plan[n])]


FIRST_UNITS = ((0, 0), (1, 0), (0, 1), (1, 1))


def quad_blocks(n, q):
    return range(4 * q, min(4 * q + 4, n % TB + 1))


def hymba_kernel(nc, x, p, norm_pre, norm_post, w_in, b_f, w_pool, pool_scale, w_out, w_pg, w_pe, ramp, out):
    with ExitStack() as ctx:
        def sem(name):
            return ctx.enter_context(nc.semaphore(name))

        def psum(name, shape):
            return ctx.enter_context(nc.psum_tensor(name, shape, F32))

        base = nc.sbuf_base
        end = nc.sbuf_usable_end
        place = [(base + 31) // 32 * 32]

        def at(name, shape, dt, offset):
            n = 2 if dt == BF16 else 4
            for d in shape[1:]:
                n *= d
            n = (n + 31) // 32 * 32
            assert offset + n <= end, (name, offset + n, end)
            return nc.alloc_sbuf_tensor_at(name, shape, dt, offset=offset), offset + n

        def sb(name, shape, dt=F32):
            t, place[0] = at(name, shape, dt, place[0])
            return t

        hn_at = place[0]
        hn_h = sb("hn_h", [P, KB, S], F32R)
        hn_l = sb("hn_l", [P, KB, S], F32R)
        w_raw = sb("w_raw", [P, 2, KB, P])
        w_h = sb("w_h", [P, 2, KB, P], F32R)
        w_l = sb("w_l", [P, 2, KB, P], F32R)
        gate = sb("gate", [P, 2, S])
        vT = sb("vT", [P, S])
        ident = sb("ident", [P, P])
        ident_b = sb("ident_b", [P, P], BF16)
        mask_b = sb("mask_b", [P, P], BF16)
        ones = sb("ones", [P, P])
        gpost = sb("gpost", [P, KB])
        pscale = sb("pscale", [P, KB])
        ramp_sb = sb("ramp_sb", [P, GROUPS, PAD])
        bf_sb = sb("bf_sb", [HEADS, 1])
        ssq = sb("ssq", [P, TB])
        rms = sb("rms", [P, TB])
        rinv = sb("rinv", [P, TB])
        eps_sb = sb("eps_sb", [P, 1])
        wait_sb = sb("wait_sb", [P, 1])
        wait_pool = sb("wait_pool", [P, 2])
        neg_max = sb("neg_max", [P, 3])
        den = sb("den", [P, 3])
        rden = sb("rden", [P, 3])
        pv_tmp = sb("pv_tmp", [P, 2, 2 * P])
        pe_raw = sb("pe_raw", [P, 2, PB, P])
        pe_h = sb("pe_h", [P, 2, PB, P], F32R)
        pe_l = sb("pe_l", [P, 2, PB, P], F32R)
        region = place[0]
        q_st, k_st = [], []
        for i in range(2):
            q_st.append(sb(f"q_st{i}", [P, 2, S], F32R))
            k_st.append(sb(f"k_st{i}", [P, 2, S], F32R))
        region2 = place[0]
        k_sw = sb("k_sw", [P, 2, S], F32R)
        pt_h = [sb("pt0_h", [P, 6, 2 * P], F32R), None]
        pt_l = [sb("pt0_l", [P, 6, 2 * P], F32R), None]
        pt_h[1] = sb("pt1_h", [P, 8, 2 * P], F32R)
        pt_l[1] = sb("pt1_l", [P, 8, 2 * P], F32R)
        v_s = sb("v_s", [P, TB, 2, P], F32R)
        e_sb = sb("e_sb", [P, 3, S + PAD])
        cb = sb("cb", [P, 2, S])
        x_all, _ = at("x_all", [P, TB, D], F32, region)
        pooled_h = pt_h[1][:].rearrange("p b c -> p (b c)").rearrange("p (c s) -> p c s", c=2)
        pooled_l = pt_l[1][:].rearrange("p b c -> p (b c)").rearrange("p (c s) -> p c s", c=2)
        wp_h = pt_h[0][:, 0:2, :]
        wp_l = pt_l[0][:, 0:2, :]
        wp_raw = cb[:, 1, 0:2 * 256].rearrange("p (c n) -> p c n", c=2)
        g_pre = cb[:, 0, :]
        mixed, o = at("mixed", [P, KB, S], F32, region)
        assert o == region2
        at_h, o = at("at_h", [P, KB, S], F32R, region2)
        at_l, _ = at("at_l", [P, KB, S], F32R, o)
        xT, o = at("xT", [P, KB, S], F32, hn_at)
        x_raw, o2 = at("x_raw", [P, 2, D], F32, o)
        p_raw, _ = at("p_raw", [P, TB // 2, PLE], F32, o2)
        hn_l_raw, _ = at("hn_l_raw", [P, KB, S], F32, o)
        at_l_raw, _ = at("at_l_raw", [P, KB, S], F32, region2 + 4 * KB * S)
        pT_h = hn_l[:, 4:6]
        pT_l = hn_l[:, 6:8]

        mix_dram = nc.dram_tensor("mix_scratch", [2 * KB, P, S], F32).ap()
        c8_dram = nc.dram_tensor("c8_scratch", [HEADS, S], F32).ap()

        pj = psum("pj", [P, 2, HALF])
        ps = psum("ps", [P, 2, S])
        pt = psum("pt", [P, 4, P])
        pv = psum("pv", [P, 2, 2 * P])
        pv_bank = pv[:].rearrange("p a (b c) -> p (a b) c", c=P)
        ps_bank = ps[:].rearrange("p a (b c) -> p (a b) c", c=HALF)

        g_in = sem("g_in")
        small_in = sem("small_in")
        x_in = [sem(f"x_in{i}") for i in range(TB)]
        raw_in = [sem("raw_in0"), sem("raw_in1")]
        wp_in = sem("wp_in")
        cb_in = [sem("cb_in0"), sem("cb_in1")]
        c8_stored = sem("c8_stored")
        gate_stored = [sem("gate_stored0"), sem("gate_stored1")]
        mix_in = [sem(f"mix_in{i}") for i in range(KB)]
        ksw_in = [sem("ksw_in0"), sem("ksw_in1")]
        xr_in = [sem("xr_in0"), sem("xr_in1")]
        p_in = sem("p_in")
        pe_in = [sem("pe_in0"), sem("pe_in1")]
        out_stored = [sem("out_stored0"), sem("out_stored1")]
        consts = sem("consts")
        eps_set = sem("eps_set")
        ssq_done = sem("ssq_done")
        rms_done = sem("rms_done")
        rinv_done = sem("rinv_done")
        xs_done = sem("xs_done")
        xt_ready = sem("xt_ready")
        xt_hi = sem("xt_hi")
        xt_lo = sem("xt_lo")
        w_hi_done = sem("w_hi_done")
        w_lo_done = sem("w_lo_done")
        wp_hi = sem("wp_hi")
        wp_lo = sem("wp_lo")
        pj_ready = sem("pj_ready")
        pj_hi = sem("pj_hi")
        pj_free = sem("pj_free")
        z_tanh = sem("z_tanh")
        pscale_half = sem("pscale_half")
        f_steps = sem("f_steps")
        f_act = sem("f_act")
        c8_ready = sem("c8_ready")
        pool_steps = sem("pool_steps")
        pooled = sem("pooled")
        lin_ready = sem("lin_ready")
        lin_gated = sem("lin_gated")
        s_ready = sem("s_ready")
        s_shifted = sem("s_shifted")
        e_done = sem("e_done")
        rden_done = sem("rden_done")
        p_ready = sem("p_ready")
        t_ready = sem("t_ready")
        t_hi = sem("t_hi")
        t_lo = sem("t_lo")
        pv_ready = sem("pv_ready")
        pv_copied = sem("pv_copied")
        pv_added = sem("pv_added")
        attn_gated = sem("attn_gated")
        mix_hi = sem("mix_hi")
        mix_lo_even = sem("mix_lo_even")
        mix_lo_odd = sem("mix_lo_odd")
        sum_zeroed = sem("sum_zeroed")
        squared = sem("squared")
        sq_summed = sem("sq_summed")
        ssum_ready = sem("ssum_ready")
        rr_done = sem("rr_done")
        rr_inv = sem("rr_inv")
        diag_done = sem("diag_done")
        rr_spread = sem("rr_spread")
        xr_t = sem("xr_t")
        xr_done = sem("xr_done")
        p_t = sem("p_t")
        p_hi = sem("p_hi")
        p_lo = sem("p_lo")
        h_scaled = sem("h_scaled")
        h_added = sem("h_added")
        h_hi = sem("h_hi")
        h_lo = sem("h_lo")
        pe_hi = sem("pe_hi")
        pe_lo = sem("pe_lo")
        gp_ready = sem("gp_ready")
        sig_done = sem("sig_done")
        gp_mul = sem("gp_mul")
        oT_done = sem("oT_done")
        oT_t = sem("oT_t")
        ost_done = sem("ost_done")


        def f32(t):
            return t.bitcast(F32)

        def half(h):
            return slice(h * HALF, (h + 1) * HALF)

        def chunk_col(job, c, pool):
            if pool:
                return job * 256 + ((COL_U if c < 2 else COL_ZP) + P * (c % 2))
            return job * P + (COL_Z, COL_Q, COL_K, COL_V)[c]

        block = ctx.enter_context(nc.Block())

        @block.sync
        def _(sp):
            def load_w(slot, src, split):
                if split is not None:
                    sp.wait_ge(w_lo_done, split)
                sp.dma_start(w_raw[:, slot], src.rearrange("(k p) c -> p k c", p=P)).then_inc(raw_in[slot], 16)

            def load_in(job, c, pool):
                m = (job if pool else job + GROUPS) * 4 + (1 + c)
                split = m - 1 if pool else None if c == 1 else m if c == 0 else m - 1
                load_w((1 + c) % 2, w_in[0, :, bass.ds(chunk_col(job, c, pool), P)], split)

            def load_out(j):
                rows = slice(D, 2 * D) if j < KB else slice(0, D)
                load_w((1 + j) % 2, w_out[0, rows, (j % KB) * P:(j % KB + 1) * P], 4 * JOB_OUT_POOL + j)

            def load_pg(db, par):
                load_w((1 + par) % 2, w_pg[0, :, bass.ds(db * P, P)], db + 4 * JOB_PG)

            sp.dma_start(x_all[:, 0], x[0, 0:P]).then_inc(x_in[0], 16)
            sp.dma_start(g_pre, norm_pre[0:1, :].broadcast_to([P, D])).then_inc(g_in, 16)
            for i in range(1, TB):
                sp.dma_start(x_all[:, i], x[0, i * P:(i + 1) * P]).then_inc(x_in[i], 16)
            load_w(0, w_in[0, :, COL_F:COL_F + P], None)
            load_w(1, w_in[0, :, COL_U:COL_U + P], None)
            with nc.allow_non_contiguous_dma(reason="a few KB of vectors"):
                sp.dma_start(bf_sb[:], b_f.rearrange("a h -> h a")).then_inc(small_in, 16)
                sp.dma_start(ramp_sb[:], ramp).then_inc(small_in, 16)
                sp.dma_start(pscale[:], pool_scale[0].rearrange("(k p) -> p k", p=P)).then_inc(small_in, 16)
                sp.dma_start(gpost[:], norm_post[0].rearrange("(k p) -> p k", p=P)).then_inc(small_in, 16)

            def load_wp(g):
                sp.dma_start(wp_raw, w_pool[0, bass.ds(g, 1)].rearrange("g (c p) n -> p (g c) n", p=P)).then_inc(wp_in, 16)

            def store_pool(g):
                for dc in range(2):
                    sp.wait_ge(lin_gated, g * 4 + (2 * dc + 2))
                    sp.dma_start(mix_dram[bass.ds(g * 2 + (KB + dc), 1)].rearrange("a p s -> (a p) s"),
                                 gate[:, dc]).then_inc(gate_stored[dc], 16)

            load_wp(0)
            load_in(0, 1, True)
            load_in(0, 2, True)
            load_in(0, 3, True)
            sp.wait_ge(c8_ready, 1)
            sp.dma_start(c8_dram, vT[0:HEADS, :]).then_inc(c8_stored, 16)
            load_in(1, 0, True)
            load_in(1, 1, True)

            def pool_loads(g, last):
                sp.wait_ge(wp_lo, g)
                load_wp(g)
                store_pool(g - 1)
                load_in(g, 2, True)
                load_in(g, 3, True)
                for c in range(2):
                    load_in(0 if last else g + 1, c, not last)

            with sp.Fori(1, GROUPS - 1) as g:
                pool_loads(g, False)
            pool_loads(GROUPS - 1, True)
            store_pool(GROUPS - 1)
            load_in(0, 2, False)
            load_in(0, 3, False)

            def load_cb(pair, hd):
                sp.dma_start(cb[:, hd], c8_dram[bass.ds(pair * 2 + hd, 1), :].broadcast_to([P, S]))\
                  .then_inc(cb_in[hd], 16)

            sp.wait_ge(c8_stored, 16)
            sp.wait_ge(xs_done, TB)
            load_cb(0, 0)
            sp.wait_ge(wp_lo, GROUPS)
            load_cb(0, 1)
            load_in(1, 0, False)
            load_in(1, 1, False)

            def pair_loads(pair, par, last):
                load_in(pair + 1, 2, False)
                load_in(pair + 1, 3, False)
                sp.wait_ge(s_shifted, pair * TILES + TB)
                load_cb(pair + 1, 0)
                for c in range(2):
                    if last:
                        load_out(c)
                    else:
                        load_in(pair + 2, c, False)
                sp.wait_ge(s_shifted, pair * TILES + TILES)
                load_cb(pair + 1, 1)
                if last:
                    sp.wait_ge(pj_ready, first_half(JOB_OUT_POOL))
                    sp.wait_ge(gate_stored[0], 16 * GROUPS)
                    sp.wait_ge(gate_stored[1], 16 * GROUPS)
                    for y in range(KB):
                        sp.dma_start(hn_l_raw[:, y], mix_dram[KB + y]).then_inc(mix_in[y], 16)
                sp.wait_ge(attn_gated, pair * 8 + 8)
                sp.dma_start(mix_dram[bass.ds(pair, 1)].rearrange("a p s -> (a p) s"), gate[:, par])\
                  .then_inc(gate_stored[par], 16)

            with sp.Fori(0, 3) as a:
                pair_loads(a * 2, 0, False)
                pair_loads(a * 2 + 1, 1, False)
            pair_loads(PAIRS - 2, 0, True)
            for j in range(2, 6):
                load_out(j)
            sp.wait_ge(gate_stored[0], 16 * (GROUPS + 4))
            sp.wait_ge(gate_stored[1], 16 * (GROUPS + 3))
            sp.wait_ge(pv_ready, 8 * PAIRS)
            for y in range(KB - 1):
                sp.dma_start(at_l_raw[:, y], mix_dram[y]).then_inc(mix_in[y], 16)
            load_out(6)
            load_out(7)

            def load_p(i):
                sp.dma_start(p_raw[:], p[0, 0, i * HALF:(i + 1) * HALF].rearrange("(b t) c -> t b c", t=P)).then_inc(p_in, 16)

            def load_pe(db, par):
                sp.dma_start(pe_raw[:, par], w_pe[0, :, bass.ds(db * P, P)].rearrange("(k p) c -> p k c", p=P))\
                  .then_inc(pe_in[par], 16)

            load_out(8)
            load_out(9)
            load_pe(0, 0)
            load_pe(1, 1)
            for i in range(TB):
                sp.wait_ge(pj_ready, first_half(JOB_OUT_ATTN) + 2 * i)
                sp.dma_start(x_raw[:, i % 2], x[0, i * P:(i + 1) * P]).then_inc(xr_in[i % 2], 16)
                if i == 0:
                    load_p(0)
                if i == 4:
                    sp.wait_ge(p_t, 2)
                    load_p(1)
                if i < 6:
                    load_out(10 + i)
                else:
                    load_pg(i - 6, i - 6)

            def store_out(u, db, h, b):
                sp.wait_ge(ost_done, u + 1)
                sp.dma_start(out[0, half(h), bass.ds(db * P, P)].rearrange("(b t) c -> t b c", t=P),
                             gate[:, 1, half(b)].rearrange("p (b c) -> p b c", c=P)).then_inc(out_stored[b], 16)

            def gate_loads(db, par):
                load_pg(db + 2, par)
                sp.wait_ge(pe_lo, db + 1)
                load_pe(db + 2, par)

            gate_loads(0, 0)
            gate_loads(1, 1)
            for u, (db, h) in enumerate(FIRST_UNITS):
                store_out(u, db, h, u % 2)
                if u == 1:
                    gate_loads(2, 0)
            for db in range(2, KB):
                if db + 3 < KB:
                    gate_loads(db + 1, (db + 1) % 2)
                for h in range(2):
                    store_out(db * 2 + h, db, h, h)
            sp.wait_ge(out_stored[0], 16 * KB)
            sp.wait_ge(out_stored[1], 16 * KB)

        @block.tensor
        def _(pe):
            def three(bank, a_h, a_l, b_h, b_l, start, stop, done=None):
                pe.matmul(bank, a_h, b_h, start=start, stop=False)
                pe.matmul(bank, a_h, b_l, start=False, stop=False)
                last = pe.matmul(bank, a_l, b_h, start=False, stop=stop)
                if done is not None:
                    last.then_inc(done, 1)

            def project(slot, h, k0, k1, moving):
                m_h, m_l = moving
                for k in range(k0, k1):
                    three(pj[:, h], w_h[:, slot, k], w_l[:, slot, k], m_h[:, k, half(h)], m_l[:, k, half(h)],
                          k == 0, k == KB - 1, pj_ready if k == KB - 1 else None)

            def piece(job, c, h, k0, k1, moving=(hn_h, hn_l)):
                if k0 == 0:
                    if h == 0:
                        pe.wait_ge(w_lo_done, job * 4 + (c + 2))
                    pe.wait_ge(pj_free, job * 8 + (2 * c + h + 1))
                project((1 + c) % 2, h, k0, k1, moving)

            def transpose_quad(dst, blocks):
                for n, b in enumerate(blocks):
                    last = pe.transpose(dst[:, n, :], b, ident[:])
                return last

            pe.wait_ge(consts, 7)
            for i in range(TB):
                pe.wait_ge(xs_done, i + 1)
                for q in range(2):
                    r = 2 * i + q
                    if r >= 4:
                        pe.wait_ge(xt_lo, r - 3)
                    transpose_quad(ps_bank[:, r % 4].rearrange("p (b t) -> p b t", t=P),
                                   [x_all[:, i, (4 * q + b) * P:(4 * q + b + 1) * P] for b in range(4)])\
                        .then_inc(xt_ready, 1)
            pe.wait_ge(w_lo_done, 1)
            for h in range(2):
                pe.wait_ge(xt_lo, TB * (h + 1))
                project(0, h, 0, KB, (hn_h, hn_l))

            def linear(g):
                pe.wait_ge(pooled, g * 2 + 2)
                pe.wait_ge(wp_lo, g + 1)
                for dc in range(2):
                    for h in range(2):
                        for c in range(2):
                            three(ps_bank[:, 2 * dc + h], wp_h[:, c, dc * P:(dc + 1) * P], wp_l[:, c, dc * P:(dc + 1) * P],
                                  pooled_h[:, c, half(h)], pooled_l[:, c, half(h)], c == 0, c == 1, lin_ready if c else None)

            def job(j):
                for c in range(4):
                    for h in range(2):
                        piece(j, c, h, 0, KB)

            job(0)
            with pe.Fori(1, GROUPS) as g:
                linear(g - 1)
                job(g)
            linear(GROUPS - 1)
            job(GROUPS)
            pe.wait_ge(lin_gated, 4 * GROUPS)

            def scores(pair, par, n):
                hd, i = divmod(n, TB)
                t = slice(i * P, (i + 1) * P)
                if i == 0:
                    pe.wait_ge(ksw_in[hd], pair * 32 + 32)
                if n >= 2:
                    pe.wait_ge(s_shifted, pair * TILES + (n - 1))
                width = (i + 1) * P
                for c0 in range(0, width, HALF):
                    c1 = min(c0 + HALF, width)
                    diagonal = c1 == width
                    pe.matmul(ps[:, n % 2, c0:c1], q_st[par][:, hd, t], k_st[par][:, hd, c0:c1], start=True, stop=False)
                    pe.matmul(ps[:, n % 2, c0:c1], q_st[par][:, hd, t], k_sw[:, hd, c0:c1], start=False, stop=not diagonal)
                    if diagonal:
                        pe.matmul(ps[:, n % 2, c1 - P:c1], ident_b[:], mask_b[:], start=False, stop=True)\
                          .then_inc(s_ready, 1)

            def turn(pair, n, q):
                at_ = pair * NQUADS + QUADS[(n, q)]
                pe.wait_ge(p_ready, pair * TILES + (n + 1))
                pe.wait_ge(t_lo, at_)
                transpose_quad(pt, [e_sb[:, n % 3, b * P:(b + 1) * P] for b in quad_blocks(n, q)]).then_inc(t_ready, 1)

            def turn_v(pair, q):
                if q == 0:
                    pe.wait_ge(pj_free, pair * 8 + (2 + 8 * GROUPS + 8))
                else:
                    pe.wait_ge(t_lo, pair * NQUADS + q)
                transpose_quad(pt, [vT[:, b * P:(b + 1) * P] for b in range(4 * q, 4 * q + 4)]).then_inc(t_ready, 1)

            def values(pair, G):
                hd, g = divmod(G, TB // 2)
                last_quad = QUADS[(2 * G + 1, 1 if 2 * g + 1 >= 4 else 0)]
                pe.wait_ge(t_lo, pair * NQUADS + (last_quad + 1))
                if G >= 2:
                    pe.wait_ge(pv_added, pair * 8 + (G - 1))
                top = 2 * g + 1
                for b in range(top + 1):
                    c0 = P if b == top else 0
                    pe.matmul(pv[:, G % 2, c0:], v_s[:, b, hd], pt_h[G % 2][:, b, c0:], start=(b == 0), stop=False)
                    last = pe.matmul(pv[:, G % 2, c0:], v_s[:, b, hd], pt_l[G % 2][:, b, c0:], start=False, stop=(b == top))
                last.then_inc(pv_ready, 1)

            def attend(pair, par, plan, last=False):
                for n in range(STEPS):
                    fill = pieces(plan, n)

                    def filler():
                        if fill:
                            c, h, k0 = fill.pop(0)
                            if last and (c, h) == (0, 0):
                                pe.wait_ge(mix_lo_even, k0 // 2 + 1)
                                pe.wait_ge(mix_lo_odd, k0 // 2 + 1)
                            piece(pair + (JOB_PAIR + 1), c, h, k0, k0 + 2)
                    if n < 2:
                        turn_v(pair, n)
                    if 2 <= n < TILES + 2:
                        turn(pair, n - 2, 0)
                    if n < TILES:
                        if n == 0:
                            pe.wait_ge(pj_free, pair * 8 + (first_half(JOB_PAIR) + 6))
                        scores(pair, par, n)
                    filler()
                    if (n - 2, 1) in QUADS:
                        turn(pair, n - 2, 1)
                    while fill:
                        filler()
                    if n >= 4 and n % 2 == 0:
                        values(pair, (n - 4) // 2)

            with pe.Fori(0, 3) as a:
                attend(a * 2, 0, PLAN)
                attend(a * 2 + 1, 1, PLAN)
            attend(PAIRS - 2, 0, PLAN_EARLY)
            attend(PAIRS - 1, 1, PLAN_LATE, True)

            job(JOB_OUT_POOL + 1)
            pe.wait_ge(mix_lo_even, KB)
            pe.wait_ge(mix_lo_odd, KB)
            with pe.Fori(0, KB // 4) as a:
                for c in range(4):
                    for h in range(2):
                        piece(a + JOB_OUT_ATTN, c, h, 0, KB, (at_h, at_l))
                    pe.wait_ge(xr_in[c % 2], a * 32 + (c // 2 + 1) * 16)
                    for q in range(2):
                        transpose_quad(ps_bank[:, 2 * (c % 2) + q].rearrange("p (b t) -> p b t", t=P),
                                       [x_raw[:, c % 2, (4 * q + b) * P:(4 * q + b + 1) * P] for b in range(4)])\
                            .then_inc(xr_t, 1)
                    if c in (1, 2):
                        if c == 1:
                            pe.wait_ge(p_in, a * 16 + 16)
                        transpose_quad((pt[:], pv_bank)[c - 1], [p_raw[:, b, (c - 1) * P:c * P] for b in range(4)])\
                            .then_inc(p_t, 1)

            def embed(db, par, h, done=None):
                bank = ps_bank[:, 2 * par + h]
                if h == 0:
                    pe.wait_ge(pe_lo, db + 1)
                for k in range(PB):
                    three(bank, pe_h[:, par, k], pe_l[:, par, k], pT_h[:, k, half(h)], pT_l[:, k, half(h)],
                          k == 0, k == PB - 1, done if k == PB - 1 else None)

            pe.wait_ge(xr_done, 2 * TB)
            pe.wait_ge(p_lo, 4)
            embed(0, 0, 0)
            for h in range(2):
                pe.wait_ge(sq_summed, 2 * KB - 1 + h)
                for i in range(4 * h, 4 * h + 4):
                    last = pe.matmul(pj[:, h, i:i + 1], gate[:, 1, i * P:(i + 1) * P], ones[:, 0:1], start=True, stop=True)
                last.then_inc(ssum_ready, 1)
                embed(0, 0, 1) if h == 0 else embed(1, 1, 0)
            for h in range(2):
                pe.wait_ge(diag_done, h + 1)
                pe.matmul((pt[:], pv_bank)[h].rearrange("p b t -> p (b t)"), ones[:], gate[:, 0, half(h)], start=True, stop=True)\
                  .then_inc(rr_spread, 1)
            embed(1, 1, 1)

            def gate_half(slot, h, b, first=False, done=None):
                for k in range(KB):
                    if first:
                        pe.wait_ge(h_lo, h * KB + k + 1)
                    three(pj[:, b], w_h[:, slot, k], w_l[:, slot, k], at_h[:, k, half(h)], at_l[:, k, half(h)],
                          k == 0, k == KB - 1, done if k == KB - 1 else None)

            def turn_out(u, b, first=False):
                pe.wait_ge(oT_done, u + 1)
                if not first:
                    pe.wait_ge(ost_done, u - 1)
                transpose_quad((pt[:], pv_bank)[b], [gate[:, 0, b * HALF + i * P:b * HALF + (i + 1) * P] for i in range(4)])\
                    .then_inc(oT_t, 1)

            for u, (db, h) in enumerate(FIRST_UNITS):
                if u < 2:
                    pe.wait_ge(w_lo_done, 4 * JOB_PG + 2 + db)
                else:
                    pe.wait_ge(sig_done, u - 1)
                gate_half((1 + db) % 2, h, u % 2, db == 0, gp_ready)
                if u >= 2:
                    turn_out(u - 2, u % 2, True)
            with pe.Fori(1, KB // 2) as a:
                for par in range(2):
                    for h in range(2):
                        u = a * 4 + (2 * par + h)
                        if h == 0:
                            pe.wait_ge(w_lo_done, a * 2 + (4 * JOB_PG + 2 + par))
                        pe.wait_ge(sig_done, u - 1)
                        gate_half((1 + par) % 2, h, h)
                        pe.wait_ge(gp_mul, u - 3)
                        embed(a * 2 + par, par, h, gp_ready)
                        turn_out(u - 2, h)
            turn_out(2 * KB - 2, 0)
            turn_out(2 * KB - 1, 1)

        @block.scalar
        def _(act):
            def split_hi(slot, loads):
                act.wait_ge(raw_in[slot], loads * 16)
                act.activation(w_h[:, slot], w_raw[:, slot], ACT.Copy).then_inc(w_hi_done, 1)

            def split_next(job, c):
                act.wait_ge(pj_ready, job * 8 + (2 * c + 2))
                split_hi(c % 2, job * 2 + (c // 2 + 2))

            def x_quads(i):
                for q in range(2):
                    r = 2 * i + q
                    act.wait_ge(xt_ready, r + 1)
                    act.activation(hn_h[:, 4 * q:4 * q + 4, i * P:(i + 1) * P],
                                   ps_bank[:, r % 4].rearrange("p (b t) -> p b t", t=P), ACT.Copy).then_inc(xt_hi, 1)

            act.wait_ge(eps_set, 1)
            for i in range(TB):
                act.wait_ge(x_in[i], 16)
                act.activation(vT[:], x_all[:, i], ACT.Square, accum_out=ssq[:, i:i + 1]).then_inc(ssq_done, 1)
                act.wait_ge(ssq_done, i + 1)
                act.activation(rms[:, i:i + 1], ssq[:, i:i + 1], ACT.Sqrt, bias=eps_sb[:], scale=1.0 / D).then_inc(rms_done, 1)
                if i == 1:
                    split_hi(0, 1)
                if i >= 2:
                    x_quads(i - 2)
            x_quads(TB - 2)
            x_quads(TB - 1)
            split_hi(1, 1)
            act.wait_ge(pj_free, 2)
            act.activation(gate[0:HEADS, 1], gate[0:HEADS, 0], ACT.Abs).then_inc(f_act, 1)
            act.wait_ge(f_act, 1)
            act.activation(gate[0:HEADS, 1], gate[0:HEADS, 1], ACT.Exp, scale=-1.0).then_inc(f_act, 1)
            act.wait_ge(f_act, 2)
            act.activation(gate[0:HEADS, 1], gate[0:HEADS, 1], ACT.Ln, bias=1.0).then_inc(f_act, 1)

            def z_half(job, c, h, dst):
                act.wait_ge(pj_ready, job * 8 + (3 + 2 * c + h))
                act.activation(dst, pj[:, h], ACT.Tanh, scale=0.5).then_inc(z_tanh, 1)

            def pool_job(g, first=False):
                for c in range(4):
                    split_next(g, c)
                    if c == 0:
                        act.wait_ge(wp_in, g * 16 + 16)
                        if not first:
                            act.wait_ge(lin_ready, g * 4)
                        act.activation(wp_h, wp_raw, ACT.Copy).then_inc(wp_hi, 1)
                    if c >= 2:
                        if first:
                            act.wait_ge(c8_ready, 1)
                        else:
                            act.wait_ge(gate_stored[c - 2], g * 16)
                        for h in range(2):
                            z_half(g, c, h, gate[:, c - 2, half(h)])

            pool_job(0, True)
            with act.Fori(1, GROUPS) as g:
                pool_job(g)

            def evacuate(pair, par, stored, c, h):
                if c == 0 and h == 0:
                    act.wait_ge(gate_stored[par], stored * 16)
                if c == 0:
                    z_half(pair + JOB_PAIR, c, h, gate[:, par, half(h)])
                elif c < 3:
                    act.wait_ge(pj_ready, pair * 8 + (first_half(JOB_PAIR) + 1 + 2 * c + h))
                    for hd in range(2):
                        rows = slice(DH * hd, DH * hd + DH)
                        act.activation((q_st, k_st)[c - 1][par][rows, hd, half(h)], pj[rows, h], ACT.Copy).then_inc(pj_hi, 1)

            for c in range(4):
                split_next(GROUPS, c)
                for h in range(2):
                    evacuate(0, 0, GROUPS, c, h)

            def quad_hi(pair, n, q):
                act.wait_ge(t_ready, pair * NQUADS + (QUADS[(n, q)] + 1))
                G = n // 2
                if G >= 2 and n % 2 == 0 and q == 0:
                    act.wait_ge(pv_ready, pair * 8 + (G - 1))
                bs = quad_blocks(n, q)
                act.activation(pt_h[G % 2][:, bs[0]:bs[-1] + 1, (n % 2) * P:(n % 2 + 1) * P], pt[:, 0:len(bs)], ACT.Copy)\
                   .then_inc(t_hi, 1)

            def v_hi(pair, q):
                act.wait_ge(t_ready, pair * NQUADS + (q + 1))
                act.activation(v_s[:, 4 * q:4 * q + 4, :, 0:DH], pt[:].rearrange("p b (h d) -> p b h d", h=2), ACT.Copy)\
                   .then_inc(t_hi, 1)

            def exps(pair, n):
                act.wait_ge(s_shifted, pair * TILES + (n + 1))
                e = e_sb[:, n % 3, 0:(n % TB + 1) * P]
                act.activation(e, e, ACT.Exp, bias=neg_max[:, n % 3:n % 3 + 1], scale=-1.0,
                               accum_out=den[:, n % 3:n % 3 + 1]).then_inc(e_done, 1)

            def v_copy(pair, G):
                hd = G // 4
                act.wait_ge(pv_ready, pair * 8 + (G + 1))
                if G >= 2:
                    act.wait_ge(attn_gated, pair * 8 + (G - 1))
                act.activation(pv_tmp[DH * hd:DH * hd + DH, G % 2], pv[DH * (1 - hd):DH * (1 - hd) + DH, G % 2], ACT.Copy)\
                   .then_inc(pv_copied, 1)

            def mix_part(y, e):
                if e and y == KB - 1:
                    act.wait_ge(attn_gated, 8 * PAIRS)
                    act.activation(at_h[:, y], gate[:, 1], ACT.Copy).then_inc(mix_hi, 1)
                else:
                    act.wait_ge(mix_in[y], 16 * (e + 1))
                    m_h, raw = ((hn_h, hn_l_raw), (at_h, at_l_raw))[e]
                    act.activation(m_h[:, y], raw[:, y], ACT.Copy).then_inc(mix_hi, 1)

            def out_copy_pool(c, h, job):
                act.wait_ge(pj_ready, first_half(job) + 2 * c + h + 1)
                act.activation(mixed[:, 4 * (job - JOB_OUT_POOL) + c, half(h)], pj[:, h], ACT.Copy).then_inc(pj_free, 1)

            def attend(pair, nxt, par, stored, plan, last=False):
                for n in range(STEPS):
                    fill = pieces(plan, n)
                    if last and n < 4:
                        mix_part(2 * n, 0)
                        mix_part(2 * n + 1, 0)
                    for c, h, k0 in fill:
                        if (h, k0) == (0, 0):
                            split_next(pair + (JOB_PAIR + 1), c)
                    if n < 2:
                        v_hi(pair, n)
                    if 2 <= n < TILES + 2:
                        quad_hi(pair, n - 2, 0)
                    if n < TILES:
                        exps(pair, n)
                    if (n - 2, 1) in QUADS:
                        quad_hi(pair, n - 2, 1)
                    for c, h, k0 in fill:
                        if k0 == KB - 2:
                            if last:
                                out_copy_pool(c, h, JOB_OUT_POOL)
                            else:
                                evacuate(nxt, 1 - par, stored, c, h)
                    if n >= 4 and n % 2 == 0:
                        v_copy(pair, (n - 4) // 2)

            with act.Fori(0, 3) as a:
                attend(a * 2, a * 2 + 1, 0, a + GROUPS, PLAN)
                attend(a * 2 + 1, a * 2 + 2, 1, a + (GROUPS + 1), PLAN)
            attend(PAIRS - 2, PAIRS - 1, 0, 3 + GROUPS, PLAN_EARLY)
            attend(PAIRS - 1, None, 1, None, PLAN_LATE, True)

            for c in range(4):
                split_next(JOB_OUT_POOL + 1, c)
                for y in range(3 * c, min(3 * c + 3, KB)):
                    mix_part(y, 1)
                for h in range(2):
                    out_copy_pool(c, h, JOB_OUT_POOL + 1)
            with act.Fori(0, KB // 4) as a:
                for c in range(4):
                    split_next(a + JOB_OUT_ATTN, c)
                    for q in range(2):
                        act.wait_ge(xr_t, a * 8 + (2 * c + q + 1))
                        act.activation(xT[:, 4 * q:4 * q + 4, bass.ds(a * HALF + c * P, P)],
                                       ps_bank[:, 2 * (c % 2) + q].rearrange("p (b t) -> p b t", t=P), ACT.Copy)\
                           .then_inc(xr_done, 1)
                    if c in (1, 2):
                        act.wait_ge(p_t, a * 2 + c)
                        act.activation(pT_h[:, c - 1, bass.ds(a * HALF, HALF)].rearrange("p (b t) -> p b t", t=P),
                                       (pt[:], pv_bank)[c - 1], ACT.Copy).then_inc(p_hi, 1)

            def split_pg(par, loads):
                split_hi((1 + par) % 2, loads)

            def pe_part(par, loads):
                act.wait_ge(pe_in[par], loads * 16)
                act.activation(pe_h[:, par], pe_raw[:, par], ACT.Copy).then_inc(pe_hi, 1)

            pe_part(0, 1)
            pe_part(1, 1)
            act.wait_ge(pj_ready, first_half(JOB_PG))
            split_pg(1, 2 * JOB_PG + 2)
            for h in range(2):
                act.wait_ge(ssum_ready, h + 1)
                act.activation(rms[:, 4 * h:4 * h + 4], pj[:, h, 4 * h:4 * h + 4], ACT.Sqrt, bias=eps_sb[:], scale=1.0 / D)\
                   .then_inc(rr_done, 1)
            for n in range(2 * KB):
                h, k = divmod(n, KB)
                act.wait_ge(h_added, n + 1)
                act.activation(at_h[:, k, half(h)], mixed[:, k, half(h)], ACT.Copy).then_inc(h_hi, 1)

            def sigmoid(u, b, first=False):
                act.wait_ge(gp_ready, u + 1)
                if not first:
                    act.wait_ge(oT_t, u - 1)
                act.activation(gate[:, 0, half(b)], pj[:, b], ACT.Sigmoid).then_inc(sig_done, 1)

            def out_copy(u, b, first=False):
                act.wait_ge(oT_t, u + 1)
                if not first:
                    act.wait_ge(out_stored[b], u * 8 - 8 * b)
                act.activation(gate[:, 1, half(b)].rearrange("p (b c) -> p b c", c=P), (pt[:], pv_bank)[b], ACT.Copy)\
                   .then_inc(ost_done, 1)

            sigmoid(0, 0, True)
            sigmoid(1, 1, True)
            sigmoid(2, 0)
            split_pg(0, 2 * JOB_PG + 2)
            pe_part(0, 2)
            out_copy(0, 0, True)
            sigmoid(3, 1)
            split_pg(1, 2 * JOB_PG + 3)
            pe_part(1, 2)
            out_copy(1, 1, True)

            def gate_block(a, par, more):
                for h in range(2):
                    u = a * 4 + (2 * par + h)
                    sigmoid(u, h)
                    if h and more:
                        split_pg(par, a + (2 * JOB_PG + 2 + par))
                        pe_part(par, a + 2)
                    out_copy(u - 2, h)

            with act.Fori(1, KB // 2 - 1) as a:
                gate_block(a, 0, True)
                gate_block(a, 1, True)
            gate_block(KB // 2 - 1, 0, False)
            gate_block(KB // 2 - 1, 1, False)
            out_copy(2 * KB - 2, 0)
            out_copy(2 * KB - 1, 1)

        @block.gpsimd
        def _(pool):
            pool.memset(ident[:], 0.0).then_inc(consts, 1)
            pool.memset(ident_b[:], 0.0).then_inc(consts, 1)
            pool.memset(mask_b[:], 0.0).then_inc(consts, 1)
            pool.memset(ones[:], 1.0).then_inc(consts, 1)
            pool.wait_ge(consts, 4)
            for t in (ident, ident_b):
                pool.affine_select(out=t[:], in_=t[:], compare_op=ALU.not_equal, fill=1.0, base=0,
                                   pattern=[[-1, P]], channel_multiplier=1).then_inc(consts, 1)
            pool.affine_select(out=mask_b[:], in_=mask_b[:], compare_op=ALU.is_ge, fill=MASKED, base=0,
                               pattern=[[-1, P]], channel_multiplier=1).then_inc(consts, 1)

            def lo(slot, m):
                pool.wait_ge(w_hi_done, m + 1)
                pool.tensor_tensor(w_l[:, slot], w_raw[:, slot], f32(w_h[:, slot]), ALU.subtract).then_inc(w_lo_done, 1)

            lo(0, 0)
            lo(1, 1)

            def job_lo(j, c):
                lo(c % 2, j * 4 + (c + 2))

            def pool_job(g):
                job_lo(g, 0)
                pool.wait_ge(wp_hi, g + 1)
                pool.tensor_tensor(wp_l, wp_raw, f32(wp_h), ALU.subtract).then_inc(wp_lo, 1)
                for c in range(1, 4):
                    job_lo(g, c)

            with pool.Fori(0, GROUPS) as g:
                pool_job(g)
            def swap_k(par, hd):
                pool.dma_start(k_sw[DH:P, hd], k_st[par][0:DH, hd]).then_inc(ksw_in[hd], 16)
                pool.dma_start(k_sw[0:DH, hd], k_st[par][DH:P, hd]).then_inc(ksw_in[hd], 16)

            def pair_weights(pair, par):
                for c in range(4):
                    job_lo(pair + (JOB_PAIR + 1), c)
                pool.wait_ge(pj_free, pair * 8 + (first_half(JOB_PAIR + 1) + 6))
                pool.wait_ge(s_ready, pair * TILES + TB)
                pool.tensor_tensor(wait_pool[:, 0:1], ones[:, 0:1], ones[:, 0:1], ALU.subtract)
                swap_k(1 - par, 0)
                pool.wait_ge(s_ready, pair * TILES + TILES)
                pool.tensor_tensor(wait_pool[:, 1:2], ones[:, 0:1], ones[:, 0:1], ALU.subtract)
                swap_k(1 - par, 1)

            for c in range(4):
                job_lo(JOB_PAIR, c)
            pool.wait_ge(pj_free, first_half(JOB_PAIR) + 6)
            swap_k(0, 0)
            swap_k(0, 1)
            with pool.Fori(0, 3) as a:
                pair_weights(a * 2, 0)
                pair_weights(a * 2 + 1, 1)
            pair_weights(PAIRS - 2, 0)

            def mix_low(y, e):
                pool.wait_ge(mix_hi, KB * e + y + 1)
                m_h, m_l, raw = ((hn_h, hn_l, hn_l_raw), (at_h, at_l, at_l_raw))[e]
                pool.tensor_tensor(m_l[:, y], raw[:, y], f32(m_h[:, y]), ALU.subtract).then_inc(mix_lo_even, 1)

            for y in range(0, KB, 2):
                mix_low(y, 0)
            for c in range(4):
                job_lo(JOB_OUT_POOL, c)
            for c in range(4):
                job_lo(JOB_OUT_POOL + 1, c)
                for y in range(3 * c, min(3 * c + 3, KB)):
                    if y % 2 == 0:
                        mix_low(y, 1)
            with pool.Fori(JOB_OUT_ATTN, JOB_PG) as j:
                for c in range(4):
                    job_lo(j, c)

            def pe_low(par, db):
                pool.wait_ge(pe_hi, db + 1)
                pool.tensor_tensor(pe_l[:, par], pe_raw[:, par], f32(pe_h[:, par]), ALU.subtract).then_inc(pe_lo, 1)

            pe_low(0, 0)
            pe_low(1, 1)
            lo(0, 4 * JOB_PG + 2)
            for n in range(2 * KB):
                h, k = divmod(n, KB)
                pool.wait_ge(h_scaled, n + 1)
                pool.tensor_tensor(mixed[:, k, half(h)], mixed[:, k, half(h)], xT[:, k, half(h)], ALU.add).then_inc(h_added, 1)
            with pool.Fori(1, KB // 2) as a:
                for par in range(2):
                    lo((1 + par) % 2, a * 2 + (4 * JOB_PG + 1 + par))
                    pe_low(par, a * 2 + par)

        @block.vector
        def _(dve):
            def x_quads(i):
                for q in range(2):
                    r = 2 * i + q
                    dve.wait_ge(xt_hi, r + 1)
                    cols = slice(i * P, (i + 1) * P)
                    dve.tensor_tensor(hn_l[:, 4 * q:4 * q + 4, cols], ps_bank[:, r % 4].rearrange("p (b t) -> p b t", t=P),
                                      f32(hn_h[:, 4 * q:4 * q + 4, cols]), ALU.subtract).then_inc(xt_lo, 1)

            dve.memset(eps_sb[:], EPS).then_inc(eps_set, 1)
            for i in range(TB):
                dve.wait_ge(rms_done, i + 1)
                dve.reciprocal(rinv[:, i:i + 1], rms[:, i:i + 1]).then_inc(rinv_done, 1)
                dve.wait_ge(rinv_done, i + 1)
                if i == 0:
                    dve.wait_ge(g_in, 16)
                dve.scalar_tensor_tensor(out=x_all[:, i], in0=x_all[:, i], scalar=rinv[:, i:i + 1], in1=g_pre,
                                         op0=ALU.mult, op1=ALU.mult).then_inc(xs_done, 1)
                if i >= 2:
                    x_quads(i - 2)
            x_quads(TB - 2)
            x_quads(TB - 1)

            dve.wait_ge(small_in, 64)
            dve.tensor_scalar(pscale[:], pscale[:], 0.5, None, ALU.mult).then_inc(pscale_half, 1)
            for h in range(2):
                dve.wait_ge(pj_ready, h + 1)
                if h == 0:
                    dve.wait_ge(ssq_done, TB)
                dve.tensor_scalar(gate[0:HEADS, 0, half(h)], pj[0:HEADS, h], bf_sb[:], -1.0, ALU.add, ALU.mult)\
                   .then_inc(pj_free, 1)
            dve.memset(e_sb[:, 1, 0:PAD], 0.0).then_inc(f_steps, 1)
            dve.wait_ge(f_act, 3)
            dve.scalar_tensor_tensor(out=gate[0:HEADS, 1], in0=gate[0:HEADS, 0], scalar=0.0, in1=gate[0:HEADS, 1],
                                     op0=ALU.max, op1=ALU.add).then_inc(f_steps, 1)
            dve.wait_ge(f_steps, 2)
            dve.wait_ge(consts, 4)
            dve.tensor_tensor_scan(vT[0:HEADS, :], ones[0:HEADS, 0:1].broadcast_to([HEADS, S]), gate[0:HEADS, 1], 0.0,
                                   ALU.mult, ALU.add).then_inc(f_steps, 1)
            dve.wait_ge(f_steps, 3)
            dve.tensor_scalar(vT[0:HEADS, :], vT[0:HEADS, :], 1.0 / SCALE, None, ALU.mult).then_inc(c8_ready, 1)

            def z_half(dst, h, index):
                dve.wait_ge(z_tanh, index + 1)
                dve.scalar_tensor_tensor(out=dst, in0=dst, scalar=1.0, in1=pj[:, h], op0=ALU.add, op1=ALU.mult)\
                   .then_inc(pj_free, 1)

            def gate_linear(g):
                dve.wait_ge(pj_free, 8 * g + 10)
                if g == 0:
                    dve.wait_ge(pscale_half, 1)
                for dc in range(2):
                    for h in range(2):
                        n = 4 * g + 2 * dc + h
                        dve.wait_ge(lin_ready, n + 1)
                        dve.scalar_tensor_tensor(out=gate[:, dc, half(h)], in0=ps_bank[:, 2 * dc + h],
                                                 scalar=pscale[:, 2 * g + dc:2 * g + dc + 1], in1=gate[:, dc, half(h)],
                                                 op0=ALU.mult, op1=ALU.mult).then_inc(lin_gated, 1)

            steps = [0]

            def then(ins):
                ins.then_inc(pool_steps, 1)
                steps[0] += 1

            def pool_window(g, c):
                w = WINDOWS[g]
                u, sums, win = e_sb[:, 0, 0:S], e_sb[:, 1], e_sb[:, 2, 0:S]
                dve.wait_ge(pj_free, 8 * g + 4 + 2 * c)
                if (g, c) == (0, 0):
                    dve.wait_ge(f_steps, 1)
                then(dve.tensor_tensor_scan(sums[:, PAD:], ones[:, 0:1].broadcast_to([P, S]), u, 0.0, ALU.mult, ALU.add))
                dve.wait_ge(pool_steps, steps[0])
                then(dve.tensor_tensor(win, sums[:, PAD:], sums[:, PAD - w:PAD - w + S], ALU.subtract))
                dve.wait_ge(pool_steps, steps[0])
                then(dve.tensor_tensor(win[:, 0:PAD], win[:, 0:PAD], ramp_sb[:, g], ALU.mult))
                dve.wait_ge(pool_steps, steps[0])
                then(dve.scalar_tensor_tensor(out=win, in0=win, scalar=1.0 / w, in1=u, op0=ALU.mult, op1=ALU.subtract))
                dve.wait_ge(pool_steps, steps[0])
                if g > 0:
                    dve.wait_ge(lin_ready, 4 * g)
                then(dve.tensor_copy(pooled_h[:, c], win))
                dve.wait_ge(pool_steps, steps[0])
                dve.tensor_tensor(pooled_l[:, c], win, f32(pooled_h[:, c]), ALU.subtract).then_inc(pooled, 1)

            for g in range(GROUPS):
                if g:
                    gate_linear(g - 1)
                for c in range(4):
                    for h in range(2):
                        if c < 2:
                            dve.wait_ge(pj_ready, 8 * g + 3 + 2 * c + h)
                            dve.tensor_copy(e_sb[:, 0, half(h)], pj[:, h]).then_inc(pj_free, 1)
                        else:
                            z_half(gate[:, c - 2, half(h)], h, 4 * g + 2 * (c - 2) + h)
                    if c < 2:
                        pool_window(g, c)
            gate_linear(GROUPS - 1)

            def evacuate(pair, par, c, h):
                if c == 0:
                    z_half(gate[:, par, half(h)], h, pair * 2 + (4 * GROUPS + h))
                elif c < 3:
                    st = (q_st, k_st)[c - 1][par]
                    for hd in range(2):
                        rows, other = slice(DH * hd, DH * hd + DH), slice(DH * (1 - hd), DH * (1 - hd) + DH)
                        dve.wait_ge(pj_hi, pair * 8 + (4 * c + 2 * h + hd - 3))
                        low = dve.tensor_tensor(st[other, hd, half(h)], pj[rows, h], f32(st[rows, hd, half(h)]), ALU.subtract)
                    low.then_inc(pj_free, 1)
                else:
                    dve.wait_ge(pj_ready, pair * 8 + (8 * GROUPS + 9 + h))
                    dve.tensor_copy(vT[:, half(h)], pj[:, h]).then_inc(pj_free, 1)

            dve.wait_ge(c8_stored, 16)
            for c in range(4):
                for h in range(2):
                    evacuate(0, 0, c, h)

            def wait_scores(pair, n):
                if n % TB == 0:
                    dve.wait_ge(cb_in[n // TB], pair * 16 + 16)
                dve.wait_ge(s_ready, pair * TILES + (n + 1))
                dve.memset(wait_sb[:], 0.0)

            def shift(pair, n):
                hd, w = n // TB, (n % TB + 1) * P
                dve.tensor_tensor_reduce(e_sb[:, n % 3, 0:w], ps[:, n % 2, 0:w], cb[:, hd, 0:w], -SCALE, 3e38,
                                         ALU.add, ALU.min, neg_max[:, n % 3:n % 3 + 1]).then_inc(s_shifted, 1)

            def normalise(pair, n):
                s = slice(n % 3, n % 3 + 1)
                e = e_sb[:, n % 3, 0:(n % TB + 1) * P]
                dve.wait_ge(e_done, pair * TILES + (n + 1))
                dve.reciprocal(rden[:, s], den[:, s]).then_inc(rden_done, 1)
                dve.wait_ge(rden_done, pair * TILES + (n + 1))
                dve.tensor_scalar(e, e, rden[:, s], 0.5, ALU.mult, ALU.mult).then_inc(p_ready, 1)

            def quad_lo(pair, n, q):
                G, bs = n // 2, quad_blocks(n, q)
                at_ = (slice(None), slice(bs[0], bs[-1] + 1), slice((n % 2) * P, (n % 2 + 1) * P))
                dve.wait_ge(t_hi, pair * NQUADS + (QUADS[(n, q)] + 1))
                dve.tensor_tensor(pt_l[G % 2][at_], pt[:, 0:len(bs)], f32(pt_h[G % 2][at_]), ALU.subtract)\
                   .then_inc(t_lo, 1)

            def v_lo(pair, q):
                dve.wait_ge(t_hi, pair * NQUADS + (q + 1))
                dve.tensor_tensor(v_s[:, 4 * q:4 * q + 4, :, DH:P], pt[:].rearrange("p b (h d) -> p b h d", h=2),
                                  f32(v_s[:, 4 * q:4 * q + 4, :, 0:DH]), ALU.subtract).then_inc(t_lo, 1)

            def add_and_gate(pair, par, G):
                hd = G // 4
                rows = slice(DH * hd, DH * hd + DH)
                cols = slice((G % 4) * 2 * P, (G % 4 + 1) * 2 * P)
                dve.wait_ge(pv_copied, pair * 8 + (G + 1))
                dve.tensor_tensor(pv_tmp[rows, G % 2], pv[rows, G % 2], pv_tmp[rows, G % 2], ALU.add).then_inc(pv_added, 1)
                dve.wait_ge(pv_added, pair * 8 + (G + 1))
                dve.tensor_tensor(gate[rows, par, cols], gate[rows, par, cols], pv_tmp[rows, G % 2], ALU.mult)\
                   .then_inc(attn_gated, 1)

            def mix_low(y, e):
                dve.wait_ge(mix_hi, KB * e + y + 1)
                m_h, m_l, raw = ((hn_h, hn_l, hn_l_raw), (at_h, at_l, at_l_raw))[e]
                src = gate[:, 1] if e and y == KB - 1 else raw[:, y]
                dve.tensor_tensor(m_l[:, y], src, f32(m_h[:, y]), ALU.subtract).then_inc(mix_lo_odd, 1)

            def attend(pair, nxt, par, plan, last=False):
                for n in range(STEPS):
                    if last and n < 4:
                        mix_low(2 * n + 1, 0)
                    if 1 <= n <= TILES:
                        normalise(pair, n - 1)
                    if n < 2:
                        v_lo(pair, n)
                    if 2 <= n < TILES + 2:
                        quad_lo(pair, n - 2, 0)
                    if n < TILES:
                        wait_scores(pair, n)
                        shift(pair, n)
                    if (n - 2, 1) in QUADS:
                        quad_lo(pair, n - 2, 1)
                    if n >= 4 and n % 2 == 0:
                        add_and_gate(pair, par, (n - 4) // 2)
                    for c, h, k0 in [] if last else pieces(plan, n):
                        if k0 == KB - 2:
                            evacuate(nxt, 1 - par, c, h)

            with dve.Fori(0, 3) as a:
                attend(a * 2, a * 2 + 1, 0, PLAN)
                attend(a * 2 + 1, a * 2 + 2, 1, PLAN)
            attend(PAIRS - 2, PAIRS - 1, 0, PLAN_EARLY)
            attend(PAIRS - 1, None, 1, PLAN_LATE, True)

            for y in range(1, KB, 2):
                mix_low(y, 1)

            dve.wait_ge(mix_lo_odd, KB)
            dve.memset(gate[:, 1], 0.0).then_inc(sum_zeroed, 1)
            dve.wait_ge(sum_zeroed, 1)
            dve.wait_ge(pj_free, first_half(JOB_OUT_ATTN))

            def p_low(c, a):
                dve.wait_ge(p_hi, a * 2 + c)
                cols = bass.ds(a * HALF, HALF)
                dve.tensor_tensor(pT_l[:, c - 1, cols].rearrange("p (b t) -> p b t", t=P), (pt[:], pv_bank)[c - 1],
                                  f32(pT_h[:, c - 1, cols]).rearrange("p (b t) -> p b t", t=P), ALU.subtract)\
                   .then_inc(p_lo, 1)

            with dve.Fori(0, KB // 4) as a:
                for c in range(4):
                    for h in range(2):
                        n = a * 8 + (2 * c + h)
                        m = mixed[:, bass.ds(a * 4 + c, 1), half(h)].rearrange("p a s -> p (a s)")
                        dve.wait_ge(pj_ready, n + (first_half(JOB_OUT_ATTN) + 1))
                        dve.tensor_tensor(m, pj[:, h], m, ALU.add).then_inc(pj_free, 1)
                        dve.wait_ge(pj_free, n + (first_half(JOB_OUT_ATTN) + 1))
                        dve.tensor_tensor(vT[:, half(h)], m, m, ALU.mult).then_inc(squared, 1)
                        dve.wait_ge(squared, n + 1)
                        dve.tensor_tensor(gate[:, 1, half(h)], gate[:, 1, half(h)], vT[:, half(h)], ALU.add)\
                           .then_inc(sq_summed, 1)
                    if c in (1, 2):
                        p_low(c, a)

            for h in range(2):
                dve.wait_ge(rr_done, h + 1)
                dve.reciprocal(rinv[:, 4 * h:4 * h + 4], rms[:, 4 * h:4 * h + 4]).then_inc(rr_inv, 1)
                dve.wait_ge(rr_inv, h + 1)
                for i in range(4 * h, 4 * h + 4):
                    last = dve.tensor_scalar(gate[:, 0, i * P:(i + 1) * P], ident[:], rinv[:, i:i + 1], None, ALU.mult)
                last.then_inc(diag_done, 1)

            def scale(n):
                h, k = divmod(n, KB)
                if k == 0:
                    dve.wait_ge(rr_spread, h + 1)
                dve.scalar_tensor_tensor(out=mixed[:, k, half(h)], in0=mixed[:, k, half(h)], scalar=gpost[:, k:k + 1],
                                         in1=(pt[:], pv_bank)[h].rearrange("p b t -> p (b t)"),
                                         op0=ALU.mult, op1=ALU.mult).then_inc(h_scaled, 1)

            def h_low(n):
                h, k = divmod(n, KB)
                dve.wait_ge(h_hi, n + 1)
                dve.tensor_tensor(at_l[:, k, half(h)], mixed[:, k, half(h)], f32(at_h[:, k, half(h)]), ALU.subtract)\
                   .then_inc(h_lo, 1)

            for n in range(2 * KB + 2):
                if n < 2 * KB:
                    scale(n)
                if n >= 2:
                    h_low(n - 2)

            def finish(u, db, par, h, b):
                g = gate[:, 0, half(b)]
                dve.wait_ge(sig_done, u + 1)
                dve.tensor_tensor(g, ps_bank[:, 2 * par + h], g, ALU.mult).then_inc(gp_mul, 1)
                dve.wait_ge(gp_mul, u + 1)
                dve.tensor_tensor(g, g, mixed[:, bass.ds(db, 1), half(h)].rearrange("p a s -> p (a s)"), ALU.add)\
                   .then_inc(oT_done, 1)

            for u, (db, h) in enumerate(FIRST_UNITS):
                finish(u, db, db, h, u % 2)
            with dve.Fori(1, KB // 2) as a:
                for par in range(2):
                    for h in range(2):
                        finish(a * 4 + (2 * par + h), a * 2 + par, par, h, h)


_INS = ["x", "p", "norm_pre", "norm_post", "w_in", "b_f", "w_pool", "pool_scale", "w_out", "w_pg", "w_pe"]


def kernel(**inputs):
    import numpy as np
    import concourse.bacc as bacc
    from concourse import mybir as mb
    from concourse.bass_utils import run_bass_kernel_spmd

    nc = bacc.Bacc("TRN2", target_bir_lowering=False, num_devices=1)
    arrays, args = {}, []
    for name in _INS:
        a = np.ascontiguousarray(inputs[name])
        arrays[f"in_{name}"] = a
        args.append(nc.dram_tensor(f"in_{name}", a.shape, mb.dt.from_np(a.dtype), kind="ExternalInput").ap())
    ramp = np.ones((128, 4, 16), np.float32)
    for g, w in enumerate((2, 4, 8, 16)):
        ramp[:, g, :w] = np.float32(w) / np.arange(1, w + 1, dtype=np.float32)
    arrays["in_ramp"] = ramp
    args.append(nc.dram_tensor("in_ramp", ramp.shape, mb.dt.float32, kind="ExternalInput").ap())
    args.append(nc.dram_tensor("out_0", (1, 1024, 1024), mb.dt.float32, kind="ExternalOutput").ap())
    hymba_kernel(nc, *args)
    r = run_bass_kernel_spmd(nc, [arrays], core_ids=[0])
    return r.results[0]["out_0"]
```

```python
from contextlib import ExitStack

import concourse.bass as bass
from concourse import mybir

F32 = mybir.dt.float32
F32R = mybir.dt.float32r
BF16 = mybir.dt.bfloat16
ACT = mybir.ActivationFunctionType
ALU = mybir.AluOpType

P = 128
D = 1024
S = 1024
KB = D // P
TB = S // P
HALF = 512
HEADS = 16
DH = 64
PAIRS = HEADS // 2
WINDOWS = (2, 4, 8, 16)
GROUPS = len(WINDOWS)
PAD = max(WINDOWS)
PLE = 256
PB = PLE // P
EPS = 1e-6
SCALE = DH ** -0.5
MASKED = -1e30

COL_Q, COL_K, COL_V, COL_Z = 0, D, 2 * D, 3 * D
COL_F = 4 * D
COL_U = COL_F + HEADS
COL_ZP = COL_U + D

JOB_PAIR = GROUPS
JOB_OUT_POOL = JOB_PAIR + PAIRS
JOB_OUT_ATTN = JOB_OUT_POOL + KB // 4
JOB_PG = JOB_OUT_ATTN + KB // 4


def first_half(job):
    return 2 + 8 * job


TILES = 2 * TB
STEPS = TILES + 3
QUADS = {}
for _n in range(TILES):
    for _q in range(1 if _n % TB < 4 else 2):
        QUADS[(_n, _q)] = 2 + len(QUADS)
NQUADS = 2 + len(QUADS)
PLAN = [2, 2, 2, 1, 1, 1, 2, 2, 2, 2, 1, 1, 1, 2, 2, 2, 2, 2, 2]
PLAN_LATE = [1, 2, 2, 2, 1, 1, 2, 2, 2, 2, 1, 1, 1, 2, 2, 2, 2, 2, 2]
for _plan in (PLAN, PLAN_LATE):
    assert len(_plan) == STEPS and sum(_plan) == 4 * 2 * (KB // 2)


def quad_first(n):
    return (n - 2, 1) in QUADS


def pieces(plan, n):
    at = sum(plan[:n])
    return [(i // 8, i // 4 % 2, 2 * (i % 4)) for i in range(at, at + plan[n])]


FIRST_UNITS = ((0, 0), (1, 0), (0, 1), (1, 1))


def mix_blocks(n):
    at = 4 * (n + 1)
    return [divmod(i, KB) for i in range(at, min(at + 4, 2 * KB))]


def quad_blocks(n, q):
    return range(4 * q, min(4 * q + 4, n % TB + 1))


def hymba_kernel(nc, x, p, norm_pre, norm_post, w_in, b_f, w_pool, pool_scale, w_out, w_pg, w_pe, ramp, out):
    with ExitStack() as ctx:
        def sem(name):
            return ctx.enter_context(nc.semaphore(name))

        def psum(name, shape):
            return ctx.enter_context(nc.psum_tensor(name, shape, F32))

        base = nc.sbuf_base
        end = nc.sbuf_usable_end
        place = [(base + 31) // 32 * 32]

        def at(name, shape, dt, offset):
            n = 2 if dt == BF16 else 4
            for d in shape[1:]:
                n *= d
            n = (n + 31) // 32 * 32
            assert offset + n <= end, (name, offset + n, end)
            return nc.alloc_sbuf_tensor_at(name, shape, dt, offset=offset), offset + n

        def sb(name, shape, dt=F32):
            t, place[0] = at(name, shape, dt, place[0])
            return t

        hn_at = place[0]
        hn_h = sb("hn_h", [P, KB, S], F32R)
        hn_l = sb("hn_l", [P, KB, S], F32R)
        w_raw = sb("w_raw", [P, 2, KB, P])
        w_h = sb("w_h", [P, 2, KB, P], F32R)
        w_l = sb("w_l", [P, 2, KB, P], F32R)
        gate = sb("gate", [P, 2, S])
        vT = sb("vT", [P, S])
        ident = sb("ident", [P, P])
        ident_b = sb("ident_b", [P, P], BF16)
        mask_b = sb("mask_b", [P, P], BF16)
        ones = sb("ones", [P, P])
        gpost = sb("gpost", [P, KB])
        pscale = sb("pscale", [P, KB])
        ramp_sb = sb("ramp_sb", [P, GROUPS, PAD])
        bf_sb = sb("bf_sb", [HEADS, 1])
        ssq = sb("ssq", [P, TB])
        rms = sb("rms", [P, TB])
        rinv = sb("rinv", [P, TB])
        eps_sb = sb("eps_sb", [P, 1])
        wait_sb = sb("wait_sb", [P, 1])
        wait_act = sb("wait_act", [P, 1])
        wait_pool = sb("wait_pool", [P, 2])
        neg_max = sb("neg_max", [P, 3])
        den = sb("den", [P, 3])
        rden = sb("rden", [P, 3])
        pv_tmp = sb("pv_tmp", [P, 2, 2 * P])
        pe_raw = sb("pe_raw", [P, 2, PB, P])
        pe_h = sb("pe_h", [P, 2, PB, P], F32R)
        pe_l = sb("pe_l", [P, 2, PB, P], F32R)
        region = place[0]
        q_st, k_st = [], []
        for i in range(2):
            q_st.append(sb(f"q_st{i}", [P, 2, S], F32R))
            k_st.append(sb(f"k_st{i}", [P, 2, S], F32R))
        region2 = place[0]
        k_sw = sb("k_sw", [P, 2, S], F32R)
        pt_h = [sb("pt0_h", [P, 6, 2 * P], F32R), None]
        pt_l = [sb("pt0_l", [P, 6, 2 * P], F32R), None]
        pt_h[1] = sb("pt1_h", [P, 8, 2 * P], F32R)
        pt_l[1] = sb("pt1_l", [P, 8, 2 * P], F32R)
        v_s = sb("v_s", [P, TB, 2, P], F32R)
        e_sb = sb("e_sb", [P, 3, S + PAD])
        cb = sb("cb", [P, 2, S])
        x_all, _ = at("x_all", [P, TB, D], F32, region)
        xg, _ = at("xg", [P, TB // 2, D], F32, region2)
        pooled_h = pt_h[1][:].rearrange("p b c -> p (b c)").rearrange("p (c s) -> p c s", c=2)
        pooled_l = pt_l[1][:].rearrange("p b c -> p (b c)").rearrange("p (c s) -> p c s", c=2)
        wp_h = pt_h[0][:, 0:2, :]
        wp_l = pt_l[0][:, 0:2, :]
        wp_raw = cb[:, 1, 0:2 * 256].rearrange("p (c n) -> p c n", c=2)
        g_pre = cb[:, 0, :]
        mixed, o = at("mixed", [P, KB, S], F32, region)
        assert o == region2
        at_h, o = at("at_h", [P, KB, S], F32R, region2)
        at_l, _ = at("at_l", [P, KB, S], F32R, o)
        xT, o = at("xT", [P, KB, S], F32, hn_at)
        x_raw, o2 = at("x_raw", [P, 2, D], F32, o)
        p_raw, _ = at("p_raw", [P, TB // 2, PLE], F32, o2)
        hn_l_raw, _ = at("hn_l_raw", [P, KB, S], F32, o)
        at_l_raw, _ = at("at_l_raw", [P, KB, S], F32, region2 + 4 * KB * S)
        pT_h = hn_l[:, 4:6]
        pT_l = hn_l[:, 6:8]

        mix_dram = nc.dram_tensor("mix_scratch", [2 * KB, P, S], F32).ap()
        c8_dram = nc.dram_tensor("c8_scratch", [HEADS, S], F32).ap()

        pj = psum("pj", [P, 2, HALF])
        ps = psum("ps", [P, 2, S])
        pt = psum("pt", [P, 4, P])
        pv = psum("pv", [P, 2, 2 * P])
        pv_bank = pv[:].rearrange("p a (b c) -> p (a b) c", c=P)
        ps_bank = ps[:].rearrange("p a (b c) -> p (a b) c", c=HALF)

        g_in = sem("g_in")
        small_in = sem("small_in")
        x_in = [sem(f"x_in{i}") for i in range(TB)]
        raw_in = [sem("raw_in0"), sem("raw_in1")]
        wp_in = sem("wp_in")
        cb_in = [sem("cb_in0"), sem("cb_in1")]
        c8_stored = sem("c8_stored")
        gate_stored = [sem("gate_stored0"), sem("gate_stored1")]
        mix_in = [[sem(f"mix_in{e}_{i}") for i in range(KB)] for e in range(2)]
        ksw_in = [sem("ksw_in0"), sem("ksw_in1")]
        xr_in = [sem("xr_in0"), sem("xr_in1")]
        p_in = sem("p_in")
        pe_in = [sem("pe_in0"), sem("pe_in1")]
        out_stored = [sem("out_stored0"), sem("out_stored1")]
        consts = sem("consts")
        eps_set = sem("eps_set")
        ssq_done = sem("ssq_done")
        xg_done = sem("xg_done")
        rms_done = sem("rms_done")
        rinv_done = sem("rinv_done")
        xs_done = sem("xs_done")
        xt_ready = sem("xt_ready")
        xt_hi = sem("xt_hi")
        xt_lo = sem("xt_lo")
        w_hi_done = sem("w_hi_done")
        w_lo_done = sem("w_lo_done")
        wp_hi = sem("wp_hi")
        wp_lo = sem("wp_lo")
        pj_ready = sem("pj_ready")
        pj_hi = sem("pj_hi")
        pj_free = sem("pj_free")
        z_tanh = sem("z_tanh")
        pscale_half = sem("pscale_half")
        f_steps = sem("f_steps")
        f_act = sem("f_act")
        c8_ready = sem("c8_ready")
        pool_steps = sem("pool_steps")
        pooled = sem("pooled")
        lin_ready = sem("lin_ready")
        lin_gated = sem("lin_gated")
        s_ready = sem("s_ready")
        s_shifted = sem("s_shifted")
        e_done = sem("e_done")
        rden_done = sem("rden_done")
        p_ready = sem("p_ready")
        t_ready = sem("t_ready")
        t_hi = sem("t_hi")
        t_lo = sem("t_lo")
        pv_ready = sem("pv_ready")
        pv_copied = sem("pv_copied")
        pv_added = sem("pv_added")
        attn_gated = sem("attn_gated")
        mix_hi = sem("mix_hi")
        mix_lo_even = sem("mix_lo_even")
        mix_lo_odd = sem("mix_lo_odd")
        sum_zeroed = sem("sum_zeroed")
        squared = sem("squared")
        sq_summed = sem("sq_summed")
        ssum_ready = sem("ssum_ready")
        rr_done = sem("rr_done")
        rr_inv = sem("rr_inv")
        diag_done = sem("diag_done")
        rr_spread = sem("rr_spread")
        xr_t = sem("xr_t")
        xr_done = sem("xr_done")
        p_t = sem("p_t")
        p_hi = sem("p_hi")
        p_lo = sem("p_lo")
        h_scaled = sem("h_scaled")
        h_added = sem("h_added")
        h_hi = sem("h_hi")
        h_lo = sem("h_lo")
        pe_hi = sem("pe_hi")
        pe_lo = sem("pe_lo")
        gp_ready = sem("gp_ready")
        sig_done = sem("sig_done")
        gp_mul = sem("gp_mul")
        oT_done = sem("oT_done")
        oT_t = sem("oT_t")
        ost_done = sem("ost_done")


        def f32(t):
            return t.bitcast(F32)

        def half(h):
            return slice(h * HALF, (h + 1) * HALF)

        def chunk_col(job, c, pool):
            if pool:
                return job * 256 + ((COL_U if c < 2 else COL_ZP) + P * (c % 2))
            return job * P + (COL_Z, COL_Q, COL_K, COL_V)[c]

        block = ctx.enter_context(nc.Block())

        @block.sync
        def _(sp):
            def load_w(slot, src, split):
                if split is not None:
                    sp.wait_ge(w_lo_done, split)
                sp.dma_start(w_raw[:, slot], src.rearrange("(k p) c -> p k c", p=P)).then_inc(raw_in[slot], 16)

            def load_in(job, c, pool):
                m = (job if pool else job + GROUPS) * 4 + (1 + c)
                split = m - 1 if pool else None if c == 1 else m if c == 0 else m - 1
                load_w((1 + c) % 2, w_in[0, :, bass.ds(chunk_col(job, c, pool), P)], split)

            def load_out(j):
                rows = slice(D, 2 * D) if j < KB else slice(0, D)
                load_w((1 + j) % 2, w_out[0, rows, (j % KB) * P:(j % KB + 1) * P], 4 * JOB_OUT_POOL + j)

            def load_pg(db, par):
                load_w((1 + par) % 2, w_pg[0, :, bass.ds(db * P, P)], db + 4 * JOB_PG)

            sp.dma_start(x_all[:, 0], x[0, 0:P]).then_inc(x_in[0], 16)
            sp.dma_start(g_pre, norm_pre[0:1, :].broadcast_to([P, D])).then_inc(g_in, 16)
            for i in range(1, TB):
                sp.dma_start(x_all[:, i], x[0, i * P:(i + 1) * P]).then_inc(x_in[i], 16)
                if i == 3:
                    load_w(0, w_in[0, :, COL_F:COL_F + P], None)
            load_w(1, w_in[0, :, COL_U:COL_U + P], None)
            with nc.allow_non_contiguous_dma(reason="a few KB of vectors"):
                sp.dma_start(bf_sb[:], b_f.rearrange("a h -> h a")).then_inc(small_in, 16)
                sp.dma_start(ramp_sb[:], ramp).then_inc(small_in, 16)
                sp.dma_start(pscale[:], pool_scale[0].rearrange("(k p) -> p k", p=P)).then_inc(small_in, 16)
                sp.dma_start(gpost[:], norm_post[0].rearrange("(k p) -> p k", p=P)).then_inc(small_in, 16)

            def load_wp(g):
                sp.dma_start(wp_raw, w_pool[0, bass.ds(g, 1)].rearrange("g (c p) n -> p (g c) n", p=P)).then_inc(wp_in, 16)

            def store_pool(g):
                for dc in range(2):
                    sp.wait_ge(lin_gated, g * 4 + (2 * dc + 2))
                    sp.dma_start(mix_dram[bass.ds(g * 2 + (KB + dc), 1)].rearrange("a p s -> (a p) s"),
                                 gate[:, dc]).then_inc(gate_stored[dc], 16)

            load_wp(0)
            load_in(0, 1, True)
            load_in(0, 2, True)
            load_in(0, 3, True)
            sp.wait_ge(c8_ready, 1)
            sp.dma_start(c8_dram, vT[0:HEADS, :]).then_inc(c8_stored, 16)
            load_in(1, 0, True)
            load_in(1, 1, True)

            def pool_loads(g, last):
                sp.wait_ge(wp_lo, g)
                load_wp(g)
                store_pool(g - 1)
                load_in(g, 2, True)
                load_in(g, 3, True)
                for c in range(2):
                    load_in(0 if last else g + 1, c, not last)

            with sp.Fori(1, GROUPS - 1) as g:
                pool_loads(g, False)
            pool_loads(GROUPS - 1, True)
            store_pool(GROUPS - 1)
            load_in(0, 2, False)
            load_in(0, 3, False)

            def load_cb(pair, hd):
                sp.dma_start(cb[:, hd], c8_dram[bass.ds(pair * 2 + hd, 1), :].broadcast_to([P, S]))\
                  .then_inc(cb_in[hd], 16)

            sp.wait_ge(c8_stored, 16)
            sp.wait_ge(xs_done, TB)
            load_cb(0, 0)
            sp.wait_ge(wp_lo, GROUPS)
            load_cb(0, 1)
            load_in(1, 0, False)
            load_in(1, 1, False)

            def pair_loads(pair, par, last):
                load_in(pair + 1, 2, False)
                load_in(pair + 1, 3, False)
                sp.wait_ge(s_shifted, pair * TILES + TB)
                load_cb(pair + 1, 0)
                for c in range(2):
                    if last:
                        load_out(c)
                    else:
                        load_in(pair + 2, c, False)
                sp.wait_ge(s_shifted, pair * TILES + TILES)
                load_cb(pair + 1, 1)
                if last:
                    sp.wait_ge(gate_stored[0], 16 * GROUPS)
                    sp.wait_ge(gate_stored[1], 16 * GROUPS)
                    for h in range(2):
                        sp.wait_ge(pj_ready, first_half(JOB_OUT_POOL) - 1 + h)
                        for y in range(KB):
                            sp.dma_start(hn_l_raw[:, y, half(h)], mix_dram[KB + y, :, half(h)]).then_inc(mix_in[h][y], 16)
                sp.wait_ge(attn_gated, pair * 8 + 8)
                sp.dma_start(mix_dram[bass.ds(pair, 1)].rearrange("a p s -> (a p) s"), gate[:, par])\
                  .then_inc(gate_stored[par], 16)

            with sp.Fori(0, 3) as a:
                pair_loads(a * 2, 0, False)
                pair_loads(a * 2 + 1, 1, False)
            pair_loads(PAIRS - 2, 0, True)
            for j in range(2, 6):
                load_out(j)
            sp.wait_ge(gate_stored[0], 16 * (GROUPS + 4))
            sp.wait_ge(gate_stored[1], 16 * (GROUPS + 3))
            sp.wait_ge(pv_ready, 8 * PAIRS)
            for y in range(KB - 1):
                sp.dma_start(at_l_raw[:, y], mix_dram[y]).then_inc(mix_in[0][y], 16)
            load_out(6)
            load_out(7)

            def load_p(i):
                sp.dma_start(p_raw[:], p[0, 0, i * HALF:(i + 1) * HALF].rearrange("(b t) c -> t b c", t=P)).then_inc(p_in, 16)

            def load_pe(db, par):
                sp.dma_start(pe_raw[:, par], w_pe[0, :, bass.ds(db * P, P)].rearrange("(k p) c -> p k c", p=P))\
                  .then_inc(pe_in[par], 16)

            load_out(8)
            load_out(9)
            load_pe(0, 0)
            load_pe(1, 1)
            for i in range(TB):
                sp.wait_ge(pj_ready, first_half(JOB_OUT_ATTN) + 2 * i)
                sp.dma_start(x_raw[:, i % 2], x[0, i * P:(i + 1) * P]).then_inc(xr_in[i % 2], 16)
                if i == 0:
                    load_p(0)
                if i == 4:
                    sp.wait_ge(p_t, 2)
                    load_p(1)
                if i < 6:
                    load_out(10 + i)
                else:
                    load_pg(i - 6, i - 6)

            def store_out(u, db, h, b):
                sp.wait_ge(ost_done, u + 1)
                sp.dma_start(out[0, half(h), bass.ds(db * P, P)].rearrange("(b t) c -> t b c", t=P),
                             gate[:, 1, half(b)].rearrange("p (b c) -> p b c", c=P)).then_inc(out_stored[b], 16)

            def gate_loads(db, par):
                load_pg(db + 2, par)
                sp.wait_ge(pe_lo, db + 1)
                load_pe(db + 2, par)

            gate_loads(0, 0)
            gate_loads(1, 1)
            for u, (db, h) in enumerate(FIRST_UNITS):
                store_out(u, db, h, u % 2)
                if u == 1:
                    gate_loads(2, 0)
            for db in range(2, KB):
                if db + 3 < KB:
                    gate_loads(db + 1, (db + 1) % 2)
                for h in range(2):
                    store_out(db * 2 + h, db, h, h)
            sp.wait_ge(out_stored[0], 16 * KB)
            sp.wait_ge(out_stored[1], 16 * KB)

        @block.tensor
        def _(pe):
            def three(bank, a_h, a_l, b_h, b_l, start, stop, done=None):
                pe.matmul(bank, a_h, b_h, start=start, stop=False)
                pe.matmul(bank, a_h, b_l, start=False, stop=False)
                last = pe.matmul(bank, a_l, b_h, start=False, stop=stop)
                if done is not None:
                    last.then_inc(done, 1)

            def project_f(h, k0, k1):
                for k in range(k0, k1):
                    three(pj[0:HEADS, h], w_h[:, 0, k, 0:HEADS], w_l[:, 0, k, 0:HEADS], hn_h[:, k, half(h)],
                          hn_l[:, k, half(h)], k == 0, k == KB - 1, pj_ready if k == KB - 1 else None)

            def project(slot, h, k0, k1, moving):
                m_h, m_l = moving
                for k in range(k0, k1):
                    three(pj[:, h], w_h[:, slot, k], w_l[:, slot, k], m_h[:, k, half(h)], m_l[:, k, half(h)],
                          k == 0, k == KB - 1, pj_ready if k == KB - 1 else None)

            def piece(job, c, h, k0, k1, moving=(hn_h, hn_l)):
                if k0 == 0:
                    if h == 0:
                        pe.wait_ge(w_lo_done, job * 4 + (c + 2))
                    pe.wait_ge(pj_free, job * 8 + (2 * c + h + 1))
                project((1 + c) % 2, h, k0, k1, moving)

            def transpose_quad(dst, blocks):
                for n, b in enumerate(blocks):
                    last = pe.transpose(dst[:, n, :], b, ident[:])
                return last

            pe.wait_ge(consts, 7)
            def turn_x(i):
                pe.wait_ge(xs_done, i + 1)
                for q in range(2):
                    r = 2 * i + q
                    if r >= 4:
                        pe.wait_ge(xt_lo, r - 3)
                    transpose_quad(ps_bank[:, r % 4].rearrange("p (b t) -> p b t", t=P),
                                   [x_all[:, i, (4 * q + b) * P:(4 * q + b + 1) * P] for b in range(4)])\
                        .then_inc(xt_ready, 1)

            for i in range(TB):
                turn_x(i)
                if i > TB // 2:
                    if i == TB // 2 + 1:
                        pe.wait_ge(w_lo_done, 1)
                        pe.wait_ge(xt_lo, TB)
                    k = 2 * (i - TB // 2 - 1)
                    project_f(0, k, k + 2)
            project_f(0, KB - 2, KB)
            pe.wait_ge(xt_lo, 2 * TB)
            project_f(1, 0, KB)

            def linear(g):
                pe.wait_ge(pooled, g * 2 + 2)
                pe.wait_ge(wp_lo, g + 1)
                for dc in range(2):
                    for h in range(2):
                        for c in range(2):
                            three(ps_bank[:, 2 * dc + h], wp_h[:, c, dc * P:(dc + 1) * P], wp_l[:, c, dc * P:(dc + 1) * P],
                                  pooled_h[:, c, half(h)], pooled_l[:, c, half(h)], c == 0, c == 1, lin_ready if c else None)

            def job(j):
                for c in range(4):
                    for h in range(2):
                        piece(j, c, h, 0, KB)

            job(0)
            with pe.Fori(1, GROUPS) as g:
                linear(g - 1)
                job(g)
            linear(GROUPS - 1)
            job(GROUPS)
            pe.wait_ge(lin_gated, 4 * GROUPS)

            def scores(pair, par, n):
                hd, i = divmod(n, TB)
                t = slice(i * P, (i + 1) * P)
                if i == 0:
                    pe.wait_ge(ksw_in[hd], pair * 32 + 32)
                if n >= 2:
                    pe.wait_ge(s_shifted, pair * TILES + (n - 1))
                width = (i + 1) * P
                for c0 in range(0, width, HALF):
                    c1 = min(c0 + HALF, width)
                    diagonal = c1 == width
                    pe.matmul(ps[:, n % 2, c0:c1], q_st[par][:, hd, t], k_st[par][:, hd, c0:c1], start=True, stop=False)
                    pe.matmul(ps[:, n % 2, c0:c1], q_st[par][:, hd, t], k_sw[:, hd, c0:c1], start=False, stop=not diagonal)
                    if diagonal:
                        pe.matmul(ps[:, n % 2, c1 - P:c1], ident_b[:], mask_b[:], start=False, stop=True)\
                          .then_inc(s_ready, 1)

            def turn(pair, n, q):
                at_ = pair * NQUADS + QUADS[(n, q)]
                pe.wait_ge(p_ready, pair * TILES + (n + 1))
                pe.wait_ge(t_lo, at_)
                transpose_quad(pt, [e_sb[:, n % 3, b * P:(b + 1) * P] for b in quad_blocks(n, q)]).then_inc(t_ready, 1)

            def turn_v(pair, q):
                if q == 0:
                    pe.wait_ge(pj_free, pair * 8 + first_half(JOB_PAIR + 1))
                else:
                    pe.wait_ge(t_lo, pair * NQUADS + q)
                transpose_quad(pt, [vT[:, b * P:(b + 1) * P] for b in range(4 * q, 4 * q + 4)]).then_inc(t_ready, 1)

            def values(pair, G):
                hd, g = divmod(G, TB // 2)
                last_quad = QUADS[(2 * G + 1, 1 if 2 * g + 1 >= 4 else 0)]
                pe.wait_ge(t_lo, pair * NQUADS + (last_quad + 1))
                if G >= 1:
                    pe.wait_ge(pv_added, pair * 8 + G)
                top = 2 * g + 1
                for b in range(top + 1):
                    c0 = P if b == top else 0
                    pe.matmul(pv[:, G % 2, c0:], v_s[:, b, hd], pt_h[G % 2][:, b, c0:], start=(b == 0), stop=False)
                    last = pe.matmul(pv[:, G % 2, c0:], v_s[:, b, hd], pt_l[G % 2][:, b, c0:], start=False, stop=(b == top))
                last.then_inc(pv_ready, 1)

            def attend(pair, par, plan, last=False):
                for n in range(STEPS):
                    fill = [(c, h, k, k + 2) for c, h, k in pieces(plan, n)]
                    if quad_first(n):
                        ahead = 3 if n % 2 == 0 or n > TILES else 2
                        fill = [(c, h, k, k + 1) for c, h, k0, k1 in fill for k in (k0, k0 + 1)]

                    def filler():
                        if fill:
                            c, h, k0, k1 = fill.pop(0)
                            if last and c == 0:
                                pe.wait_ge(mix_lo_even, h * (KB // 2) + k0 // 2 + 1)
                                pe.wait_ge(mix_lo_odd, h * (KB // 2) + k0 // 2 + 1)
                            piece(pair + (JOB_PAIR + 1), c, h, k0, k1)
                    if quad_first(n):
                        turn(pair, n - 2, 0)
                    if n < TILES:
                        if n == 0:
                            pe.wait_ge(pj_free, pair * 8 + (first_half(JOB_PAIR) + 6))
                        scores(pair, par, n)
                    if 3 <= n < TILES + 2 and not quad_first(n):
                        turn(pair, n - 2, 0)
                    for _ in range(ahead if quad_first(n) else 2 if n == 0 else 1):
                        filler()
                    if n < 2:
                        turn_v(pair, n)
                    elif n == 2:
                        turn(pair, 0, 0)
                    elif quad_first(n):
                        turn(pair, n - 2, 1)
                    elif n == STEPS - 1:
                        values(pair, (n - 4) // 2)
                    while fill:
                        filler()
                    if n >= 4 and n % 2 == 0 and n < STEPS - 1:
                        values(pair, (n - 4) // 2)

            with pe.Fori(0, 3) as a:
                attend(a * 2, 0, PLAN)
                attend(a * 2 + 1, 1, PLAN)
            attend(PAIRS - 2, 0, PLAN)
            attend(PAIRS - 1, 1, PLAN_LATE, True)

            job(JOB_OUT_POOL + 1)
            pe.wait_ge(mix_lo_even, KB + KB // 2)
            pe.wait_ge(mix_lo_odd, KB + KB // 2)
            def turn_again(a, c):
                pe.wait_ge(xr_in[c % 2], a * 32 + (c // 2 + 1) * 16)
                for q in range(2):
                    transpose_quad(ps_bank[:, 2 * (c % 2) + q].rearrange("p (b t) -> p b t", t=P),
                                   [x_raw[:, c % 2, (4 * q + b) * P:(4 * q + b + 1) * P] for b in range(4)])\
                        .then_inc(xr_t, 1)
                if c in (1, 2):
                    if c == 1:
                        pe.wait_ge(p_in, a * 16 + 16)
                    transpose_quad((pt[:], pv_bank)[c - 1], [p_raw[:, b, (c - 1) * P:c * P] for b in range(4)])\
                        .then_inc(p_t, 1)

            def sum_squares(h):
                pe.wait_ge(sq_summed, 2 * KB - 1 + h)
                for i in range(4 * h, 4 * h + 4):
                    last = pe.matmul(pj[:, h, i:i + 1], gate[:, 1, i * P:(i + 1) * P], ones[:, 0:1], start=True, stop=True)
                last.then_inc(ssum_ready, 1)

            def spread(h):
                pe.wait_ge(diag_done, h + 1)
                pe.matmul((pt[:], pv_bank)[h].rearrange("p b t -> p (b t)"), ones[:], gate[:, 0, half(h)], start=True, stop=True)\
                  .then_inc(rr_spread, 1)

            attn = (at_h, at_l)
            with pe.Fori(0, KB // 4 - 1) as a:
                for c in range(4):
                    for h in range(2):
                        piece(a + JOB_OUT_ATTN, c, h, 0, KB, attn)
                    turn_again(a, c)
            for c in range(3):
                for h in range(2):
                    piece(JOB_PG - 1, c, h, 0, KB, attn)
                turn_again(KB // 4 - 1, c)
            piece(JOB_PG - 1, 3, 0, 0, KB, attn)
            turn_again(KB // 4 - 1, 3)
            piece(JOB_PG - 1, 3, 1, 0, 3, attn)
            sum_squares(0)
            piece(JOB_PG - 1, 3, 1, 3, KB - 1, attn)
            pe.wait_ge(p_lo, 4)
            spread(0)
            piece(JOB_PG - 1, 3, 1, KB - 1, KB, attn)

            def embed(db, par, h, done=None):
                bank = ps_bank[:, 2 * par + h]
                if h == 0:
                    pe.wait_ge(pe_lo, db + 1)
                for k in range(PB):
                    three(bank, pe_h[:, par, k], pe_l[:, par, k], pT_h[:, k, half(h)], pT_l[:, k, half(h)],
                          k == 0, k == PB - 1, done if k == PB - 1 else None)

            pe.wait_ge(xr_done, 2 * TB)
            for db in range(2):
                for h in range(2):
                    embed(db, db, h)
            sum_squares(1)

            def gate_half(slot, h, b, first=False, done=None, k0=0, k1=KB):
                for k in range(k0, k1):
                    if first:
                        pe.wait_ge(h_lo, h * KB + k + 1)
                    three(pj[:, b], w_h[:, slot, k], w_l[:, slot, k], at_h[:, k, half(h)], at_l[:, k, half(h)],
                          k == 0, k == KB - 1, done if k == KB - 1 else None)

            def turn_out(u, b, first=False):
                pe.wait_ge(oT_done, u + 1)
                if not first:
                    pe.wait_ge(ost_done, u - 1)
                transpose_quad((pt[:], pv_bank)[b], [gate[:, 0, b * HALF + i * P:b * HALF + (i + 1) * P] for i in range(4)])\
                    .then_inc(oT_t, 1)

            for u, (db, h) in enumerate(FIRST_UNITS):
                if u < 2:
                    pe.wait_ge(w_lo_done, 4 * JOB_PG + 2 + db)
                else:
                    pe.wait_ge(sig_done, u - 1)
                if u == 0:
                    gate_half(1, 0, 0, True, None, 0, KB // 2)
                    spread(1)
                    gate_half(1, 0, 0, True, gp_ready, KB // 2, KB)
                else:
                    gate_half((1 + db) % 2, h, u % 2, db == 0, gp_ready)
                if u >= 2:
                    turn_out(u - 2, u % 2, True)
            with pe.Fori(1, KB // 2) as a:
                for par in range(2):
                    for h in range(2):
                        u = a * 4 + (2 * par + h)
                        if h == 0:
                            pe.wait_ge(w_lo_done, a * 2 + (4 * JOB_PG + 2 + par))
                        pe.wait_ge(sig_done, u - 1)
                        gate_half((1 + par) % 2, h, h)
                        pe.wait_ge(gp_mul, u - 3)
                        embed(a * 2 + par, par, h, gp_ready)
                        turn_out(u - 2, h)
            turn_out(2 * KB - 2, 0)
            turn_out(2 * KB - 1, 1)

        @block.scalar
        def _(act):
            def split_hi(slot, loads):
                act.wait_ge(raw_in[slot], loads * 16)
                act.activation(w_h[:, slot], w_raw[:, slot], ACT.Copy).then_inc(w_hi_done, 1)

            def split_next(job, c):
                act.wait_ge(pj_ready, job * 8 + (2 * c + 2))
                split_hi(c % 2, job * 2 + (c // 2 + 2))

            def x_quads(i):
                for q in range(2):
                    r = 2 * i + q
                    act.wait_ge(xt_ready, r + 1)
                    act.activation(hn_h[:, 4 * q:4 * q + 4, i * P:(i + 1) * P],
                                   ps_bank[:, r % 4].rearrange("p (b t) -> p b t", t=P), ACT.Copy).then_inc(xt_hi, 1)

            act.wait_ge(eps_set, 1)
            act.activation(wait_act[:], eps_sb[:], ACT.Sqrt)
            for i in range(TB):
                act.wait_ge(x_in[i], 16)
                act.activation(vT[:], x_all[:, i], ACT.Square, accum_out=ssq[:, i:i + 1]).then_inc(ssq_done, 1)
                act.wait_ge(ssq_done, i + 1)
                act.activation(rms[:, i:i + 1], ssq[:, i:i + 1], ACT.Sqrt, bias=eps_sb[:], scale=1.0 / D).then_inc(rms_done, 1)
                if i >= 2:
                    x_quads(i - 2)
                if i == 4:
                    act.wait_ge(raw_in[0], 16)
                    act.activation(w_h[:, 0, :, 0:HEADS], w_raw[:, 0, :, 0:HEADS], ACT.Copy).then_inc(w_hi_done, 1)
            x_quads(TB - 2)
            x_quads(TB - 1)
            split_hi(1, 1)
            act.wait_ge(pj_free, 2)
            act.activation(gate[0:HEADS, 1], gate[0:HEADS, 0], ACT.Abs).then_inc(f_act, 1)
            act.wait_ge(f_act, 1)
            act.activation(gate[0:HEADS, 1], gate[0:HEADS, 1], ACT.Exp, scale=-1.0).then_inc(f_act, 1)
            act.wait_ge(f_act, 2)
            act.activation(gate[0:HEADS, 1], gate[0:HEADS, 1], ACT.Ln, bias=1.0).then_inc(f_act, 1)

            def z_half(job, c, h, dst):
                act.wait_ge(pj_ready, job * 8 + (3 + 2 * c + h))
                act.activation(dst, pj[:, h], ACT.Tanh, scale=0.5).then_inc(z_tanh, 1)

            def pool_job(g, first=False):
                for c in range(4):
                    split_next(g, c)
                    if c == 0:
                        act.wait_ge(wp_in, g * 16 + 16)
                        if not first:
                            act.wait_ge(lin_ready, g * 4)
                        act.activation(wp_h, wp_raw, ACT.Copy).then_inc(wp_hi, 1)
                    if c >= 2:
                        if first:
                            act.wait_ge(c8_ready, 1)
                        else:
                            act.wait_ge(gate_stored[c - 2], g * 16)
                        for h in range(2):
                            z_half(g, c, h, gate[:, c - 2, half(h)])

            pool_job(0, True)
            with act.Fori(1, GROUPS) as g:
                pool_job(g)

            def evacuate(pair, par, stored, c, h):
                if c == 0 and h == 0:
                    act.wait_ge(gate_stored[par], stored * 16)
                if c == 0:
                    z_half(pair + JOB_PAIR, c, h, gate[:, par, half(h)])
                elif c < 3:
                    act.wait_ge(pj_ready, pair * 8 + (first_half(JOB_PAIR) + 1 + 2 * c + h))
                    for hd in range(2):
                        rows = slice(DH * hd, DH * hd + DH)
                        act.activation((q_st, k_st)[c - 1][par][rows, hd, half(h)], pj[rows, h], ACT.Copy).then_inc(pj_hi, 1)

            for c in range(4):
                split_next(GROUPS, c)
                for h in range(2):
                    evacuate(0, 0, GROUPS, c, h)

            def quad_hi(pair, n, q):
                act.wait_ge(t_ready, pair * NQUADS + (QUADS[(n, q)] + 1))
                G = n // 2
                if G >= 2 and n % 2 == 0 and q == 0:
                    act.wait_ge(pv_ready, pair * 8 + (G - 1))
                bs = quad_blocks(n, q)
                act.activation(pt_h[G % 2][:, bs[0]:bs[-1] + 1, (n % 2) * P:(n % 2 + 1) * P], pt[:, 0:len(bs)], ACT.Copy)\
                   .then_inc(t_hi, 1)

            def v_hi(pair, q):
                act.wait_ge(t_ready, pair * NQUADS + (q + 1))
                act.activation(v_s[:, 4 * q:4 * q + 4, :, 0:DH], pt[:].rearrange("p b (h d) -> p b h d", h=2), ACT.Copy)\
                   .then_inc(t_hi, 1)

            def exps(pair, n):
                act.wait_ge(s_shifted, pair * TILES + (n + 1))
                e = e_sb[:, n % 3, 0:(n % TB + 1) * P]
                act.activation(e, e, ACT.Exp, bias=neg_max[:, n % 3:n % 3 + 1], scale=-1.0,
                               accum_out=den[:, n % 3:n % 3 + 1]).then_inc(e_done, 1)

            def v_copy(pair, G):
                hd = G // 4
                act.wait_ge(pv_ready, pair * 8 + (G + 1))
                if G >= 2:
                    act.wait_ge(attn_gated, pair * 8 + (G - 1))
                act.activation(pv_tmp[DH * hd:DH * hd + DH, G % 2], pv[DH * (1 - hd):DH * (1 - hd) + DH, G % 2], ACT.Copy)\
                   .then_inc(pv_copied, 1)

            def mix_high_pool(y, h):
                act.wait_ge(mix_in[h][y], 16)
                act.activation(hn_h[:, y, half(h)], hn_l_raw[:, y, half(h)], ACT.Copy).then_inc(mix_hi, 1)

            def mix_high_attn(y):
                if y == KB - 1:
                    act.wait_ge(attn_gated, 8 * PAIRS)
                    act.activation(at_h[:, y], gate[:, 1], ACT.Copy).then_inc(mix_hi, 1)
                else:
                    act.wait_ge(mix_in[0][y], 32)
                    act.activation(at_h[:, y], at_l_raw[:, y], ACT.Copy).then_inc(mix_hi, 1)

            def out_copy_pool(c, h, job):
                act.wait_ge(pj_ready, first_half(job) + 2 * c + h + 1)
                act.activation(mixed[:, 4 * (job - JOB_OUT_POOL) + c, half(h)], pj[:, h], ACT.Copy).then_inc(pj_free, 1)

            def attend(pair, nxt, par, stored, plan, last=False):
                def finished(n):
                    for c, h, k0 in pieces(plan, n) if n >= 0 else []:
                        if k0 == KB - 2:
                            if last:
                                out_copy_pool(c, h, JOB_OUT_POOL)
                            else:
                                evacuate(nxt, 1 - par, stored, c, h)

                for n in range(STEPS):
                    fill = pieces(plan, n)
                    if 3 <= n < TILES + 2:
                        quad_hi(pair, n - 2, 0)
                    if n >= 5 and n % 2:
                        v_copy(pair, (n - 5) // 2)
                    finished(n - 1)
                    if quad_first(n):
                        quad_hi(pair, n - 2, 1)
                    if n < TILES:
                        exps(pair, n)
                    if n < 2:
                        v_hi(pair, n)
                    elif n == 2:
                        quad_hi(pair, 0, 0)
                    for h, y in mix_blocks(n) if last else []:
                        mix_high_pool(y, h)
                    for c, h, k0 in fill:
                        if (h, k0) == (0, 0):
                            split_next(pair + (JOB_PAIR + 1), c)
                v_copy(pair, (STEPS - 5) // 2)
                finished(STEPS - 1)

            with act.Fori(0, 3) as a:
                attend(a * 2, a * 2 + 1, 0, a + GROUPS, PLAN)
                attend(a * 2 + 1, a * 2 + 2, 1, a + (GROUPS + 1), PLAN)
            attend(PAIRS - 2, PAIRS - 1, 0, 3 + GROUPS, PLAN)
            for h, y in mix_blocks(-1):
                mix_high_pool(y, h)
            attend(PAIRS - 1, None, 1, None, PLAN_LATE, True)

            for c in range(4):
                split_next(JOB_OUT_POOL + 1, c)
                for y in range(3 * c, min(3 * c + 3, KB)):
                    mix_high_attn(y)
                for h in range(2):
                    out_copy_pool(c, h, JOB_OUT_POOL + 1)
            def turned_again(a, c):
                for q in range(2):
                    act.wait_ge(xr_t, a * 8 + (2 * c + q + 1))
                    act.activation(xT[:, 4 * q:4 * q + 4, bass.ds(a * HALF + c * P, P)],
                                   ps_bank[:, 2 * (c % 2) + q].rearrange("p (b t) -> p b t", t=P), ACT.Copy)\
                       .then_inc(xr_done, 1)
                if c in (1, 2):
                    act.wait_ge(p_t, a * 2 + c)
                    act.activation(pT_h[:, c - 1, bass.ds(a * HALF, HALF)].rearrange("p (b t) -> p b t", t=P),
                                   (pt[:], pv_bank)[c - 1], ACT.Copy).then_inc(p_hi, 1)

            def split_pg(par, loads):
                split_hi((1 + par) % 2, loads)

            def pe_part(par, loads):
                act.wait_ge(pe_in[par], loads * 16)
                act.activation(pe_h[:, par], pe_raw[:, par], ACT.Copy).then_inc(pe_hi, 1)

            pe_part(0, 1)
            pe_part(1, 1)
            with act.Fori(0, KB // 4) as a:
                for c in range(4):
                    split_next(a + JOB_OUT_ATTN, c)
                    turned_again(a, c)

            def root(h):
                act.wait_ge(ssum_ready, h + 1)
                act.activation(rms[:, 4 * h:4 * h + 4], pj[:, h, 4 * h:4 * h + 4], ACT.Sqrt, bias=eps_sb[:], scale=1.0 / D)\
                   .then_inc(rr_done, 1)

            act.activation(wait_act[:], eps_sb[:], ACT.Sqrt)
            root(0)

            def h_high(n):
                h, k = divmod(n, KB)
                act.wait_ge(h_added, n + 1)
                act.activation(at_h[:, k, half(h)], mixed[:, k, half(h)], ACT.Copy).then_inc(h_hi, 1)

            def sigmoid(u, b, first=False):
                act.wait_ge(gp_ready, u + 1)
                if not first:
                    act.wait_ge(oT_t, u - 1)
                act.activation(gate[:, 0, half(b)], pj[:, b], ACT.Sigmoid).then_inc(sig_done, 1)

            def out_copy(u, b, first=False):
                act.wait_ge(oT_t, u + 1)
                if not first:
                    act.wait_ge(out_stored[b], u * 8 - 8 * b)
                act.activation(gate[:, 1, half(b)].rearrange("p (b c) -> p b c", c=P), (pt[:], pv_bank)[b], ACT.Copy)\
                   .then_inc(ost_done, 1)

            for n in range(2 * KB):
                if n == 1:
                    act.wait_ge(pj_ready, first_half(JOB_PG))
                    split_pg(1, 2 * JOB_PG + 2)
                if n == 4:
                    root(1)
                h_high(n)
                if n == 8:
                    sigmoid(0, 0, True)
                if n == 12:
                    sigmoid(1, 1, True)
            sigmoid(2, 0)
            split_pg(0, 2 * JOB_PG + 2)
            pe_part(0, 2)
            out_copy(0, 0, True)
            sigmoid(3, 1)
            split_pg(1, 2 * JOB_PG + 3)
            pe_part(1, 2)
            out_copy(1, 1, True)

            def gate_block(a, par, more):
                for h in range(2):
                    u = a * 4 + (2 * par + h)
                    sigmoid(u, h)
                    if h and more:
                        split_pg(par, a + (2 * JOB_PG + 2 + par))
                        pe_part(par, a + 2)
                    out_copy(u - 2, h)

            with act.Fori(1, KB // 2 - 1) as a:
                gate_block(a, 0, True)
                gate_block(a, 1, True)
            gate_block(KB // 2 - 1, 0, False)
            gate_block(KB // 2 - 1, 1, False)
            out_copy(2 * KB - 2, 0)
            out_copy(2 * KB - 1, 1)

        @block.gpsimd
        def _(pool):
            pool.memset(ident[:], 0.0).then_inc(consts, 1)
            pool.memset(ident_b[:], 0.0).then_inc(consts, 1)
            pool.memset(mask_b[:], 0.0).then_inc(consts, 1)
            pool.memset(ones[:], 1.0).then_inc(consts, 1)
            pool.wait_ge(consts, 4)
            for t in (ident, ident_b):
                pool.affine_select(out=t[:], in_=t[:], compare_op=ALU.not_equal, fill=1.0, base=0,
                                   pattern=[[-1, P]], channel_multiplier=1).then_inc(consts, 1)
            pool.affine_select(out=mask_b[:], in_=mask_b[:], compare_op=ALU.is_ge, fill=MASKED, base=0,
                               pattern=[[-1, P]], channel_multiplier=1).then_inc(consts, 1)

            def lo(slot, m):
                pool.wait_ge(w_hi_done, m + 1)
                pool.tensor_tensor(w_l[:, slot], w_raw[:, slot], f32(w_h[:, slot]), ALU.subtract).then_inc(w_lo_done, 1)

            pool.wait_ge(g_in, 16)
            for i in range(1, TB, 2):
                pool.wait_ge(x_in[i], 16)
                pool.tensor_tensor(xg[:, i // 2], x_all[:, i], g_pre, ALU.mult).then_inc(xg_done, 1)
                if i == 5:
                    pool.wait_ge(w_hi_done, 1)
                    f_cols = (slice(None), 0, slice(None), slice(0, HEADS))
                    pool.tensor_tensor(w_l[f_cols], w_raw[f_cols], f32(w_h[f_cols]), ALU.subtract).then_inc(w_lo_done, 1)
            lo(1, 1)

            def job_lo(j, c):
                lo(c % 2, j * 4 + (c + 2))

            def pool_job(g):
                job_lo(g, 0)
                pool.wait_ge(wp_hi, g + 1)
                pool.tensor_tensor(wp_l, wp_raw, f32(wp_h), ALU.subtract).then_inc(wp_lo, 1)
                for c in range(1, 4):
                    job_lo(g, c)

            with pool.Fori(0, GROUPS) as g:
                pool_job(g)
            def swap_k(par, hd):
                pool.dma_start(k_sw[DH:P, hd], k_st[par][0:DH, hd]).then_inc(ksw_in[hd], 16)
                pool.dma_start(k_sw[0:DH, hd], k_st[par][DH:P, hd]).then_inc(ksw_in[hd], 16)

            def pair_weights(pair, par):
                for c in range(4):
                    job_lo(pair + (JOB_PAIR + 1), c)
                pool.wait_ge(pj_free, pair * 8 + (first_half(JOB_PAIR + 1) + 6))
                pool.wait_ge(s_ready, pair * TILES + TB)
                pool.tensor_tensor(wait_pool[:, 0:1], ones[:, 0:1], ones[:, 0:1], ALU.subtract)
                swap_k(1 - par, 0)
                pool.wait_ge(s_ready, pair * TILES + TILES)
                pool.tensor_tensor(wait_pool[:, 1:2], ones[:, 0:1], ones[:, 0:1], ALU.subtract)
                swap_k(1 - par, 1)

            for c in range(4):
                job_lo(JOB_PAIR, c)
            pool.wait_ge(pj_free, first_half(JOB_PAIR) + 6)
            swap_k(0, 0)
            swap_k(0, 1)
            with pool.Fori(0, 3) as a:
                pair_weights(a * 2, 0)
                pair_weights(a * 2 + 1, 1)
            pair_weights(PAIRS - 2, 0)

            def mix_low_attn(y):
                pool.wait_ge(mix_hi, 2 * KB + y + 1)
                pool.tensor_tensor(at_l[:, y], at_l_raw[:, y], f32(at_h[:, y]), ALU.subtract).then_inc(mix_lo_even, 1)

            for h in range(2):
                for y in range(0, KB, 2):
                    pool.wait_ge(mix_hi, KB * h + y + 1)
                    pool.tensor_tensor(hn_l[:, y, half(h)], hn_l_raw[:, y, half(h)], f32(hn_h[:, y, half(h)]), ALU.subtract)\
                        .then_inc(mix_lo_even, 1)
            for c in range(4):
                job_lo(JOB_OUT_POOL, c)
            for c in range(4):
                job_lo(JOB_OUT_POOL + 1, c)
                for y in range(3 * c, min(3 * c + 3, KB)):
                    if y % 2 == 0:
                        mix_low_attn(y)
            def pe_low(par, db):
                pool.wait_ge(pe_hi, db + 1)
                pool.tensor_tensor(pe_l[:, par], pe_raw[:, par], f32(pe_h[:, par]), ALU.subtract).then_inc(pe_lo, 1)

            pe_low(0, 0)
            pe_low(1, 1)
            with pool.Fori(JOB_OUT_ATTN, JOB_PG) as j:
                for c in range(4):
                    job_lo(j, c)

            for n in range(2 * KB):
                h, k = divmod(n, KB)
                if n == KB:
                    lo(0, 4 * JOB_PG + 2)
                pool.wait_ge(h_scaled, n + 1)
                pool.tensor_tensor(mixed[:, k, half(h)], mixed[:, k, half(h)], xT[:, k, half(h)], ALU.add).then_inc(h_added, 1)
            with pool.Fori(1, KB // 2) as a:
                for par in range(2):
                    lo((1 + par) % 2, a * 2 + (4 * JOB_PG + 1 + par))
                    pe_low(par, a * 2 + par)

        @block.vector
        def _(dve):
            def x_quads(i):
                for q in range(2):
                    r = 2 * i + q
                    dve.wait_ge(xt_hi, r + 1)
                    cols = slice(i * P, (i + 1) * P)
                    dve.tensor_tensor(hn_l[:, 4 * q:4 * q + 4, cols], ps_bank[:, r % 4].rearrange("p (b t) -> p b t", t=P),
                                      f32(hn_h[:, 4 * q:4 * q + 4, cols]), ALU.subtract).then_inc(xt_lo, 1)

            dve.memset(eps_sb[:], EPS).then_inc(eps_set, 1)
            for i in range(TB):
                dve.wait_ge(rms_done, i + 1)
                dve.reciprocal(rinv[:, i:i + 1], rms[:, i:i + 1]).then_inc(rinv_done, 1)
                dve.wait_ge(rinv_done, i + 1)
                if i == 0:
                    dve.wait_ge(g_in, 16)
                if i % 2:
                    dve.wait_ge(xg_done, i // 2 + 1)
                    dve.tensor_scalar(x_all[:, i], xg[:, i // 2], rinv[:, i:i + 1], None, ALU.mult).then_inc(xs_done, 1)
                else:
                    dve.scalar_tensor_tensor(out=x_all[:, i], in0=x_all[:, i], scalar=rinv[:, i:i + 1], in1=g_pre,
                                             op0=ALU.mult, op1=ALU.mult).then_inc(xs_done, 1)
                if i >= 2:
                    x_quads(i - 2)
            x_quads(TB - 2)
            x_quads(TB - 1)

            dve.wait_ge(small_in, 64)
            dve.tensor_scalar(pscale[:], pscale[:], 0.5, None, ALU.mult).then_inc(pscale_half, 1)
            for h in range(2):
                dve.wait_ge(pj_ready, h + 1)
                if h == 0:
                    dve.wait_ge(ssq_done, TB)
                dve.tensor_scalar(gate[0:HEADS, 0, half(h)], pj[0:HEADS, h], bf_sb[:], -1.0, ALU.add, ALU.mult)\
                   .then_inc(pj_free, 1)
            dve.memset(e_sb[:, 1, 0:PAD], 0.0).then_inc(f_steps, 1)
            dve.wait_ge(f_act, 3)
            dve.scalar_tensor_tensor(out=gate[0:HEADS, 1], in0=gate[0:HEADS, 0], scalar=0.0, in1=gate[0:HEADS, 1],
                                     op0=ALU.max, op1=ALU.add).then_inc(f_steps, 1)
            dve.wait_ge(f_steps, 2)
            dve.wait_ge(consts, 4)
            dve.tensor_tensor_scan(vT[0:HEADS, :], ones[0:HEADS, 0:1].broadcast_to([HEADS, S]), gate[0:HEADS, 1], 0.0,
                                   ALU.mult, ALU.add).then_inc(f_steps, 1)
            dve.wait_ge(f_steps, 3)
            dve.tensor_scalar(vT[0:HEADS, :], vT[0:HEADS, :], 1.0 / SCALE, None, ALU.mult).then_inc(c8_ready, 1)

            def z_half(dst, h, index):
                dve.wait_ge(z_tanh, index + 1)
                dve.scalar_tensor_tensor(out=dst, in0=dst, scalar=1.0, in1=pj[:, h], op0=ALU.add, op1=ALU.mult)\
                   .then_inc(pj_free, 1)

            def gate_linear(g):
                dve.wait_ge(pj_free, 8 * g + 10)
                if g == 0:
                    dve.wait_ge(pscale_half, 1)
                for dc in range(2):
                    for h in range(2):
                        n = 4 * g + 2 * dc + h
                        dve.wait_ge(lin_ready, n + 1)
                        dve.scalar_tensor_tensor(out=gate[:, dc, half(h)], in0=ps_bank[:, 2 * dc + h],
                                                 scalar=pscale[:, 2 * g + dc:2 * g + dc + 1], in1=gate[:, dc, half(h)],
                                                 op0=ALU.mult, op1=ALU.mult).then_inc(lin_gated, 1)

            steps = [0]

            def then(ins):
                ins.then_inc(pool_steps, 1)
                steps[0] += 1

            def pool_window(g, c):
                w = WINDOWS[g]
                u, sums, win = e_sb[:, 0, 0:S], e_sb[:, 1], e_sb[:, 2, 0:S]
                dve.wait_ge(pj_free, 8 * g + 4 + 2 * c)
                if (g, c) == (0, 0):
                    dve.wait_ge(f_steps, 1)
                then(dve.tensor_tensor_scan(sums[:, PAD:], ones[:, 0:1].broadcast_to([P, S]), u, 0.0, ALU.mult, ALU.add))
                dve.wait_ge(pool_steps, steps[0])
                then(dve.tensor_tensor(win, sums[:, PAD:], sums[:, PAD - w:PAD - w + S], ALU.subtract))
                dve.wait_ge(pool_steps, steps[0])
                then(dve.tensor_tensor(win[:, 0:PAD], win[:, 0:PAD], ramp_sb[:, g], ALU.mult))
                dve.wait_ge(pool_steps, steps[0])
                then(dve.scalar_tensor_tensor(out=win, in0=win, scalar=1.0 / w, in1=u, op0=ALU.mult, op1=ALU.subtract))
                dve.wait_ge(pool_steps, steps[0])
                if g > 0:
                    dve.wait_ge(lin_ready, 4 * g)
                then(dve.tensor_copy(pooled_h[:, c], win))
                dve.wait_ge(pool_steps, steps[0])
                dve.tensor_tensor(pooled_l[:, c], win, f32(pooled_h[:, c]), ALU.subtract).then_inc(pooled, 1)

            for g in range(GROUPS):
                if g:
                    gate_linear(g - 1)
                for c in range(4):
                    for h in range(2):
                        if c < 2:
                            dve.wait_ge(pj_ready, 8 * g + 3 + 2 * c + h)
                            dve.tensor_copy(e_sb[:, 0, half(h)], pj[:, h]).then_inc(pj_free, 1)
                        else:
                            z_half(gate[:, c - 2, half(h)], h, 4 * g + 2 * (c - 2) + h)
                    if c < 2:
                        pool_window(g, c)
            gate_linear(GROUPS - 1)

            def evacuate(pair, par, c, h):
                if c == 0:
                    z_half(gate[:, par, half(h)], h, pair * 2 + (4 * GROUPS + h))
                elif c < 3:
                    st = (q_st, k_st)[c - 1][par]
                    for hd in range(2):
                        rows, other = slice(DH * hd, DH * hd + DH), slice(DH * (1 - hd), DH * (1 - hd) + DH)
                        dve.wait_ge(pj_hi, pair * 8 + (4 * c + 2 * h + hd - 3))
                        low = dve.tensor_tensor(st[other, hd, half(h)], pj[rows, h], f32(st[rows, hd, half(h)]), ALU.subtract)
                    low.then_inc(pj_free, 1)
                else:
                    dve.wait_ge(pj_ready, pair * 8 + (first_half(JOB_PAIR) + 7 + h))
                    dve.tensor_copy(vT[:, half(h)], pj[:, h]).then_inc(pj_free, 1)

            dve.wait_ge(c8_stored, 16)
            for c in range(4):
                for h in range(2):
                    evacuate(0, 0, c, h)

            def wait_scores(pair, n):
                if n % TB == 0:
                    dve.wait_ge(cb_in[n // TB], pair * 16 + 16)
                dve.wait_ge(s_ready, pair * TILES + (n + 1))
                dve.memset(wait_sb[:], 0.0)

            def shift(pair, n):
                hd, w = n // TB, (n % TB + 1) * P
                dve.tensor_tensor_reduce(e_sb[:, n % 3, 0:w], ps[:, n % 2, 0:w], cb[:, hd, 0:w], -SCALE, 3e38,
                                         ALU.add, ALU.min, neg_max[:, n % 3:n % 3 + 1]).then_inc(s_shifted, 1)

            def normalise(pair, n):
                s = slice(n % 3, n % 3 + 1)
                e = e_sb[:, n % 3, 0:(n % TB + 1) * P]
                dve.wait_ge(e_done, pair * TILES + (n + 1))
                dve.reciprocal(rden[:, s], den[:, s]).then_inc(rden_done, 1)
                dve.wait_ge(rden_done, pair * TILES + (n + 1))
                dve.tensor_scalar(e, e, rden[:, s], 0.5, ALU.mult, ALU.mult).then_inc(p_ready, 1)

            def quad_lo(pair, n, q):
                G, bs = n // 2, quad_blocks(n, q)
                at_ = (slice(None), slice(bs[0], bs[-1] + 1), slice((n % 2) * P, (n % 2 + 1) * P))
                dve.wait_ge(t_hi, pair * NQUADS + (QUADS[(n, q)] + 1))
                dve.tensor_tensor(pt_l[G % 2][at_], pt[:, 0:len(bs)], f32(pt_h[G % 2][at_]), ALU.subtract)\
                   .then_inc(t_lo, 1)

            def v_lo(pair, q):
                dve.wait_ge(t_hi, pair * NQUADS + (q + 1))
                dve.tensor_tensor(v_s[:, 4 * q:4 * q + 4, :, DH:P], pt[:].rearrange("p b (h d) -> p b h d", h=2),
                                  f32(v_s[:, 4 * q:4 * q + 4, :, 0:DH]), ALU.subtract).then_inc(t_lo, 1)

            def add_and_gate(pair, par, G):
                hd = G // 4
                rows = slice(DH * hd, DH * hd + DH)
                cols = slice((G % 4) * 2 * P, (G % 4 + 1) * 2 * P)
                dve.wait_ge(pv_copied, pair * 8 + (G + 1))
                dve.tensor_tensor(pv_tmp[rows, G % 2], pv[rows, G % 2], pv_tmp[rows, G % 2], ALU.add).then_inc(pv_added, 1)
                dve.wait_ge(pv_added, pair * 8 + (G + 1))
                dve.tensor_tensor(gate[rows, par, cols], gate[rows, par, cols], pv_tmp[rows, G % 2], ALU.mult)\
                   .then_inc(attn_gated, 1)

            def mix_low_pool(y, h):
                dve.wait_ge(mix_hi, KB * h + y + 1)
                dve.tensor_tensor(hn_l[:, y, half(h)], hn_l_raw[:, y, half(h)], f32(hn_h[:, y, half(h)]), ALU.subtract)\
                   .then_inc(mix_lo_odd, 1)

            def mix_low_attn(y):
                dve.wait_ge(mix_hi, 2 * KB + y + 1)
                src = gate[:, 1] if y == KB - 1 else at_l_raw[:, y]
                dve.tensor_tensor(at_l[:, y], src, f32(at_h[:, y]), ALU.subtract).then_inc(mix_lo_odd, 1)

            def attend(pair, nxt, par, plan, last=False):
                def finished(n):
                    done = [(c, h) for c, h, k0 in pieces(plan, n) if k0 == KB - 2] if n >= 0 and not last else []
                    for c, h in done:
                        evacuate(nxt, 1 - par, c, h)
                    return done

                for n in range(STEPS):
                    if quad_first(n):
                        quad_lo(pair, n - 2, 0)
                    if n < TILES:
                        wait_scores(pair, n)
                        shift(pair, n)
                    if 3 <= n < TILES + 2 and not quad_first(n):
                        quad_lo(pair, n - 2, 0)
                    turn = n >= 5 and n % 2
                    if not finished(n - 1) and turn:
                        add_and_gate(pair, par, (n - 5) // 2)
                        turn = False
                    if quad_first(n):
                        quad_lo(pair, n - 2, 1)
                    if n < TILES:
                        normalise(pair, n)
                    if n < 2:
                        v_lo(pair, n)
                    elif n == 2:
                        quad_lo(pair, 0, 0)
                    if turn:
                        add_and_gate(pair, par, (n - 5) // 2)
                    for h, y in mix_blocks(n) if last else []:
                        if y % 2:
                            mix_low_pool(y, h)
                add_and_gate(pair, par, (STEPS - 5) // 2)
                finished(STEPS - 1)

            with dve.Fori(0, 3) as a:
                attend(a * 2, a * 2 + 1, 0, PLAN)
                attend(a * 2 + 1, a * 2 + 2, 1, PLAN)
            attend(PAIRS - 2, PAIRS - 1, 0, PLAN)
            for h, y in mix_blocks(-1):
                if y % 2:
                    mix_low_pool(y, h)
            attend(PAIRS - 1, None, 1, PLAN_LATE, True)

            for y in range(1, KB, 2):
                mix_low_attn(y)

            dve.wait_ge(mix_lo_odd, KB + KB // 2)
            dve.memset(gate[:, 1], 0.0).then_inc(sum_zeroed, 1)
            dve.wait_ge(sum_zeroed, 1)
            dve.wait_ge(pj_free, first_half(JOB_OUT_ATTN))

            def p_low(c, a):
                dve.wait_ge(p_hi, a * 2 + c)
                cols = bass.ds(a * HALF, HALF)
                dve.tensor_tensor(pT_l[:, c - 1, cols].rearrange("p (b t) -> p b t", t=P), (pt[:], pv_bank)[c - 1],
                                  f32(pT_h[:, c - 1, cols]).rearrange("p (b t) -> p b t", t=P), ALU.subtract)\
                   .then_inc(p_lo, 1)

            def out_half(a, c, h):
                n = a * 8 + (2 * c + h)
                m = mixed[:, bass.ds(a * 4 + c, 1), half(h)].rearrange("p a s -> p (a s)")
                dve.wait_ge(pj_ready, n + (first_half(JOB_OUT_ATTN) + 1))
                dve.tensor_tensor(m, pj[:, h], m, ALU.add).then_inc(pj_free, 1)
                dve.wait_ge(pj_free, n + (first_half(JOB_OUT_ATTN) + 1))
                dve.tensor_tensor(vT[:, half(h)], m, m, ALU.mult).then_inc(squared, 1)
                dve.wait_ge(squared, n + 1)
                dve.tensor_tensor(gate[:, 1, half(h)], gate[:, 1, half(h)], vT[:, half(h)], ALU.add)\
                   .then_inc(sq_summed, 1)

            def out_chunk(a, c):
                for h in range(2):
                    out_half(a, c, h)
                if c in (1, 2):
                    p_low(c, a)

            with dve.Fori(0, KB // 4 - 1) as a:
                for c in range(4):
                    out_chunk(a, c)
            for c in range(3):
                out_chunk(KB // 4 - 1, c)
            out_half(KB // 4 - 1, 3, 0)

            def inverse(h):
                dve.wait_ge(rr_done, h + 1)
                dve.reciprocal(rinv[:, 4 * h:4 * h + 4], rms[:, 4 * h:4 * h + 4]).then_inc(rr_inv, 1)
                dve.wait_ge(rr_inv, h + 1)
                for i in range(4 * h, 4 * h + 4):
                    last = dve.tensor_scalar(gate[:, 0, i * P:(i + 1) * P], ident[:], rinv[:, i:i + 1], None, ALU.mult)
                last.then_inc(diag_done, 1)

            def scale(n):
                h, k = divmod(n, KB)
                if k == 0:
                    dve.wait_ge(rr_spread, h + 1)
                dve.scalar_tensor_tensor(out=mixed[:, k, half(h)], in0=mixed[:, k, half(h)], scalar=gpost[:, k:k + 1],
                                         in1=(pt[:], pv_bank)[h].rearrange("p b t -> p (b t)"),
                                         op0=ALU.mult, op1=ALU.mult).then_inc(h_scaled, 1)

            def h_low(n):
                h, k = divmod(n, KB)
                dve.wait_ge(h_hi, n + 1)
                dve.tensor_tensor(at_l[:, k, half(h)], mixed[:, k, half(h)], f32(at_h[:, k, half(h)]), ALU.subtract)\
                   .then_inc(h_lo, 1)

            inverse(0)
            for n in range(2 * KB + 2):
                if n < 2 * KB:
                    scale(n)
                if n >= 2:
                    h_low(n - 2)
                if n == 2:
                    out_half(KB // 4 - 1, 3, 1)
                if n == 5:
                    inverse(1)

            def finish(u, db, par, h, b):
                g = gate[:, 0, half(b)]
                dve.wait_ge(sig_done, u + 1)
                dve.tensor_tensor(g, ps_bank[:, 2 * par + h], g, ALU.mult).then_inc(gp_mul, 1)
                dve.wait_ge(gp_mul, u + 1)
                dve.tensor_tensor(g, g, mixed[:, bass.ds(db, 1), half(h)].rearrange("p a s -> p (a s)"), ALU.add)\
                   .then_inc(oT_done, 1)

            for u, (db, h) in enumerate(FIRST_UNITS):
                finish(u, db, db, h, u % 2)
            with dve.Fori(1, KB // 2) as a:
                for par in range(2):
                    for h in range(2):
                        finish(a * 4 + (2 * par + h), a * 2 + par, par, h, h)


_INS = ["x", "p", "norm_pre", "norm_post", "w_in", "b_f", "w_pool", "pool_scale", "w_out", "w_pg", "w_pe"]


def kernel(**inputs):
    import numpy as np
    import concourse.bacc as bacc
    from concourse import mybir as mb
    from concourse.bass_utils import run_bass_kernel_spmd

    nc = bacc.Bacc("TRN2", target_bir_lowering=False, num_devices=1)
    arrays, args = {}, []
    for name in _INS:
        a = np.ascontiguousarray(inputs[name])
        arrays[f"in_{name}"] = a
        args.append(nc.dram_tensor(f"in_{name}", a.shape, mb.dt.from_np(a.dtype), kind="ExternalInput").ap())
    ramp = np.ones((128, 4, 16), np.float32)
    for g, w in enumerate((2, 4, 8, 16)):
        ramp[:, g, :w] = np.float32(w) / np.arange(1, w + 1, dtype=np.float32)
    arrays["in_ramp"] = ramp
    args.append(nc.dram_tensor("in_ramp", ramp.shape, mb.dt.float32, kind="ExternalInput").ap())
    args.append(nc.dram_tensor("out_0", (1, 1024, 1024), mb.dt.float32, kind="ExternalOutput").ap())
    hymba_kernel(nc, *args)
    r = run_bass_kernel_spmd(nc, [arrays], core_ids=[0])
    return r.results[0]["out_0"]
```
